# Optimizing a Trainium2 kernel written in Bass

```python
import math
import jax, jax.numpy as jnp
from jax import lax
import numpy as np

D_MODEL = 1024
BATCH = 1
SEQ = 512
DEPTH = 2

N_MIXERS = 2
SSM_GROUP = 16
SSM_GROUPS = D_MODEL // SSM_GROUP
SSM_STATE = 64
CONV_WIDTH = 3
FFN_HIDDEN = ((8 * D_MODEL + 3 * 256 - 1) // (3 * 256)) * 256
N_SSM_LAYERS = (DEPTH + 1) // 2
N_CONV_LAYERS = DEPTH // 2
RMS_EPS = 1e-6
DT_MIN = 1e-3
DT_MAX = 1e-1


def rms_norm(x, g):
    x32 = x.astype(jnp.float32)
    y = x32 * lax.rsqrt(jnp.mean(x32 * x32, axis=-1, keepdims=True) + RMS_EPS)
    return (y * g.astype(jnp.float32)).astype(x.dtype)

def modulate(h, shift, scale):
    return h * (1.0 + scale) + shift

def _ssm_combine(e1, e2):
    a1r, a1i, b1r, b1i = e1
    a2r, a2i, b2r, b2i = e2
    ar = a2r * a1r - a2i * a1i
    ai = a2r * a1i + a2i * a1r
    br = a2r * b1r - a2i * b1i + b2r
    bi = a2r * b1i + a2i * b1r + b2i
    return (ar, ai, br, bi)

def s5_mixer(h, a_re, a_im, log_step, b_re, b_im, c_re, c_im, d, w_out):
    bsz, seqlen, _ = h.shape
    f32 = jnp.float32
    u = h.astype(f32).reshape(bsz, seqlen, SSM_GROUPS, SSM_GROUP)
    lr = jnp.minimum(a_re.astype(f32), -1e-4)
    li = a_im.astype(f32)
    dt = jnp.exp(log_step.astype(f32))[:, None]
    mag = jnp.exp(lr * dt)
    abr = mag * jnp.cos(li * dt)
    abi = mag * jnp.sin(li * dt)
    den = lr * lr + li * li
    qr = ((abr - 1.0) * lr + abi * li) / den
    qi = (abi * lr - (abr - 1.0) * li) / den
    br, bim = b_re.astype(f32), b_im.astype(f32)
    bbar_re = qr[..., None] * br - qi[..., None] * bim
    bbar_im = qr[..., None] * bim + qi[..., None] * br
    bu_re = jnp.einsum('blgh,gph->blgp', u, bbar_re)
    bu_im = jnp.einsum('blgh,gph->blgp', u, bbar_im)
    a_r = jnp.broadcast_to(abr[None, None], (1, seqlen, SSM_GROUPS, SSM_STATE))
    a_i = jnp.broadcast_to(abi[None, None], (1, seqlen, SSM_GROUPS, SSM_STATE))
    _, _, xr, xi = lax.associative_scan(_ssm_combine, (a_r, a_i, bu_re, bu_im), axis=1)
    y = (jnp.einsum('ghp,blgp->blgh', c_re.astype(f32), xr)
         - jnp.einsum('ghp,blgp->blgh', c_im.astype(f32), xi))
    y = y.reshape(bsz, seqlen, D_MODEL) + d.astype(f32) * h.astype(f32)
    y = jax.nn.gelu(y).astype(h.dtype)
    val, gate = jnp.split(y @ w_out, 2, axis=-1)
    return val * jax.nn.sigmoid(gate)

def short_conv_mixer(h, w_in, conv_w, w_out):
    bg, cg, v = jnp.split(h @ w_in, 3, axis=-1)
    cv = cg * v
    conv = lax.conv_general_dilated(
        cv, conv_w[:, None, :].astype(cv.dtype), window_strides=(1,),
        padding=[(CONV_WIDTH - 1, 0)], dimension_numbers=('NWC', 'WIO', 'NWC'),
        feature_group_count=D_MODEL)
    return (bg * conv) @ w_out

def swiglu(h, w_in, w_out):
    g, u = jnp.split(h @ w_in, 2, axis=-1)
    return (jax.nn.silu(g) * u) @ w_out

def first_inputs(seed: int = 0) -> dict:
    key = jax.random.key(seed)
    ks = jax.random.split(key, 24)
    D, G, P, H, F = D_MODEL, SSM_GROUPS, SSM_STATE, SSM_GROUP, FFN_HIDDEN
    nrm = jax.random.normal
    x = nrm(ks[0], (BATCH, SEQ, D), jnp.float32)
    c = nrm(ks[1], (BATCH, D), jnp.float32)
    norm1_g = 1.0 + 0.02 * nrm(ks[2], (DEPTH, D), jnp.float32)
    norm2_g = 1.0 + 0.02 * nrm(ks[3], (DEPTH, D), jnp.float32)
    w_ada = 0.5 * D ** -0.5 * nrm(ks[4], (DEPTH, D, 6 * D), jnp.float32)
    b_ada = 0.01 * nrm(ks[5], (DEPTH, 6 * D), jnp.float32)
    n_idx = jnp.arange(P, dtype=jnp.float32)
    ssm_a_re = -0.5 + 0.01 * nrm(ks[6], (N_SSM_LAYERS, G, P), jnp.float32)
    ssm_a_im = math.pi * n_idx + 0.01 * nrm(ks[7], (N_SSM_LAYERS, G, P), jnp.float32)
    ssm_log_step = jax.random.uniform(ks[8], (N_SSM_LAYERS, G), jnp.float32,
                                      math.log(DT_MIN), math.log(DT_MAX))
    ssm_b_re = (2 * H) ** -0.5 * nrm(ks[9], (N_SSM_LAYERS, G, P, H), jnp.float32)
    ssm_b_im = (2 * H) ** -0.5 * nrm(ks[10], (N_SSM_LAYERS, G, P, H), jnp.float32)
    ssm_c_re = (2 * P) ** -0.5 * nrm(ks[11], (N_SSM_LAYERS, G, H, P), jnp.float32)
    ssm_c_im = (2 * P) ** -0.5 * nrm(ks[12], (N_SSM_LAYERS, G, H, P), jnp.float32)
    ssm_d = nrm(ks[13], (N_SSM_LAYERS, D), jnp.float32)
    ssm_w_out = D ** -0.5 * nrm(ks[14], (N_SSM_LAYERS, D, 2 * D), jnp.float32)
    conv_w_in = D ** -0.5 * nrm(ks[15], (N_CONV_LAYERS, D, 3 * D), jnp.float32)
    conv_w = CONV_WIDTH ** -0.5 * nrm(ks[16], (N_CONV_LAYERS, CONV_WIDTH, D), jnp.float32)
    conv_w_out = D ** -0.5 * nrm(ks[17], (N_CONV_LAYERS, D, D), jnp.float32)
    w_ffn_in = D ** -0.5 * nrm(ks[18], (DEPTH, D, 2 * F), jnp.float32)
    w_ffn_out = F ** -0.5 * nrm(ks[19], (DEPTH, F, D), jnp.float32)
    final_g = 1.0 + 0.02 * nrm(ks[20], (D,), jnp.float32)
    return {"x": x, "c": c, "norm1_g": norm1_g, "norm2_g": norm2_g,
            "w_ada": w_ada, "b_ada": b_ada,
            "ssm_a_re": ssm_a_re, "ssm_a_im": ssm_a_im, "ssm_log_step": ssm_log_step,
            "ssm_b_re": ssm_b_re, "ssm_b_im": ssm_b_im,
            "ssm_c_re": ssm_c_re, "ssm_c_im": ssm_c_im,
            "ssm_d": ssm_d, "ssm_w_out": ssm_w_out,
            "conv_w_in": conv_w_in, "conv_w": conv_w, "conv_w_out": conv_w_out,
            "w_ffn_in": w_ffn_in, "w_ffn_out": w_ffn_out, "final_g": final_g}

def first_block(x, c, norm1_g, norm2_g, w_ada, b_ada,
              ssm_a_re, ssm_a_im, ssm_log_step, ssm_b_re, ssm_b_im,
              ssm_c_re, ssm_c_im, ssm_d, ssm_w_out,
              conv_w_in, conv_w, conv_w_out,
              w_ffn_in, w_ffn_out, final_g):
    c_act = jax.nn.silu(c)
    for i in range(DEPTH):
        mods = c_act @ w_ada[i] + b_ada[i]
        sh1, sc1, g1, sh2, sc2, g2 = [m[:, None, :] for m in jnp.split(mods, 6, axis=-1)]
        h = modulate(rms_norm(x, norm1_g[i]), sh1, sc1)
        j = i // N_MIXERS
        if i % N_MIXERS == 0:
            mix = s5_mixer(h, ssm_a_re[j], ssm_a_im[j], ssm_log_step[j],
                           ssm_b_re[j], ssm_b_im[j], ssm_c_re[j], ssm_c_im[j],
                           ssm_d[j], ssm_w_out[j])
        else:
            mix = short_conv_mixer(h, conv_w_in[j], conv_w[j], conv_w_out[j])
        x = x + g1 * mix
        h = modulate(rms_norm(x, norm2_g[i]), sh2, sc2)
        x = x + g2 * swiglu(h, w_ffn_in[i], w_ffn_out[i])
    return rms_norm(x, final_g)


N_ATTN_LAYERS = (DEPTH + 1) // 2
N_HGRN_LAYERS = DEPTH // 2
ATTN_HEAD_DIM = 64
ATTN_HEADS = D_MODEL // ATTN_HEAD_DIM
DILATED_PATTERNS = ((128, 1), (512, 4), (2048, 16))
N_GROUPS = len(DILATED_PATTERNS)
ROPE_THETA = 10000.0
HGRN_EXPAND = 128
HGRN_HEADS = D_MODEL // HGRN_EXPAND
HGRN_DK = HGRN_EXPAND
HGRN_DV = D_MODEL // HGRN_HEADS
HGRN_CHUNK = 64
D_FF = 4 * D_MODEL
LN_EPS = 1e-5
DEEPNORM_ALPHA = (2 * DEPTH) ** 0.25
DEEPNORM_BETA = (8 * DEPTH) ** -0.25


F32 = jnp.float32

def layer_norm(x, g, b):
    xf = x.astype(F32)
    mu = jnp.mean(xf, axis=-1, keepdims=True)
    var = jnp.mean(jnp.square(xf - mu), axis=-1, keepdims=True)
    return ((xf - mu) * lax.rsqrt(var + LN_EPS) * g.astype(F32) + b.astype(F32)).astype(x.dtype)

def rotary(x, pos):
    e = x.shape[-1]
    half = e // 2
    inv = ROPE_THETA ** (-jnp.arange(half, dtype=F32) * (2.0 / e))
    ang = pos.astype(F32)[:, None] * inv[None, :]
    cos = jnp.cos(ang)[None, :, None, :]
    sin = jnp.sin(ang)[None, :, None, :]
    xf = x.astype(F32)
    x1, x2 = xf[..., :half], xf[..., half:]
    return jnp.concatenate([x1 * cos - x2 * sin, x2 * cos + x1 * sin], axis=-1).astype(x.dtype)

def dilated_window_attention(q, k, v, window, dilation):
    B, S, H, E = q.shape
    blk = window // dilation
    span = dilation * blk
    s_pad = -(-S // span) * span
    n = s_pad // dilation
    nb = n // blk
    pad = ((0, 0), (0, s_pad - S), (0, 0), (0, 0))

    def to_blocks(t):
        t = jnp.pad(t, pad).reshape(B, n, dilation, H, E).transpose(0, 2, 1, 3, 4)
        return t.reshape(B * dilation, nb, blk, H, E)

    def with_prev(t):
        prev = jnp.pad(t, ((0, 0), (1, 0), (0, 0), (0, 0), (0, 0)))[:, :-1]
        return jnp.concatenate([prev, t], axis=2)

    qb, kb, vb = to_blocks(q), to_blocks(k), to_blocks(v)
    kk, vv = with_prev(kb), with_prev(vb)
    s = jnp.einsum('znqhe,znkhe->znhqk', qb, kk).astype(F32) * (E ** -0.5)
    qi = jnp.arange(blk)[:, None]
    kj = jnp.arange(2 * blk)[None, :]
    dist = qi + blk - kj
    in_band = (dist >= 0) & (dist <= blk)
    kabs = jnp.arange(nb)[:, None, None] * blk + kj[None] - blk
    valid = in_band[None] & (kabs >= 0)
    s = jnp.where(valid[None, :, None], s, -jnp.inf)
    m = jnp.max(s, axis=-1, keepdims=True)
    p = jnp.exp(s - m)
    l = jnp.sum(p, axis=-1, keepdims=True)
    o = jnp.einsum('znhqk,znkhe->znqhe', (p / l).astype(v.dtype), vv)
    lse = (m + jnp.log(l))[..., 0].transpose(0, 1, 3, 2)

    def from_blocks(t):
        t = t.reshape(B, dilation, n, *t.shape[3:]).swapaxes(1, 2)
        return t.reshape(B, s_pad, *t.shape[3:])[:, :S]

    return from_blocks(o), from_blocks(lse)

def dilated_attention_mixer(x, w_in, w_out):
    B, S, _ = x.shape
    proj = (x @ w_in).reshape(B, S, N_GROUPS, 3, ATTN_HEADS, ATTN_HEAD_DIM)
    pos = jnp.arange(S)
    outs, lses = [], []
    for g, (window, dilation) in enumerate(DILATED_PATTERNS):
        q = rotary(proj[:, :, g, 0], pos)
        k = rotary(proj[:, :, g, 1], pos)
        o, lse = dilated_window_attention(q, k, proj[:, :, g, 2], window, dilation)
        outs.append(o)
        lses.append(lse)
    wts = jax.nn.softmax(jnp.stack(lses, axis=0), axis=0)
    o = jnp.einsum('gbsh,gbshe->bshe', wts, jnp.stack(outs, axis=0).astype(F32))
    return o.reshape(B, S, ATTN_HEADS * ATTN_HEAD_DIM).astype(x.dtype) @ w_out

def forget_lower_bounds(lb_logits):
    c = jnp.cumsum(jax.nn.softmax(lb_logits.astype(F32), axis=0), axis=0)
    return c - c[0]

def hgrn2_mixer(x, w_in, w_out, norm_g, lb):
    B, S, _ = x.shape
    H, K, V, C = HGRN_HEADS, HGRN_DK, HGRN_DV, HGRN_CHUNK
    nc = S // C
    q_raw, f_raw, i_raw = jnp.split(x @ w_in, [H * K, 2 * H * K], axis=-1)
    z = f_raw.astype(F32)
    log_f = jnp.logaddexp(jnp.log(lb), jnp.log1p(-lb) + jax.nn.log_sigmoid(z))
    key = (1.0 - lb) * jax.nn.sigmoid(-z)
    q = jax.nn.silu(q_raw.astype(F32))
    v = i_raw.astype(F32)

    def chunks(t, d):
        return t.reshape(B, nc, C, H, d).transpose(0, 3, 1, 2, 4)

    q, key, log_f, v = chunks(q, K), chunks(key, K), chunks(log_f, K), chunks(v, V)
    b = jnp.cumsum(log_f, axis=3)
    q_dec = q * jnp.exp(b)
    k_dec = key * jnp.exp(-b)
    causal = jnp.tril(jnp.ones((C, C), dtype=bool))
    a = jnp.where(causal, jnp.einsum('bhcid,bhcjd->bhcij', q_dec, k_dec), 0.0)
    o_intra = jnp.einsum('bhcij,bhcje->bhcie', a, v)
    b_last = b[:, :, :, -1:, :]
    kv = jnp.einsum('bhcjd,bhcje->bhcde', key * jnp.exp(b_last - b), v)
    chunk_decay = jnp.exp(b_last[:, :, :, 0, :])

    def step(state, inp):
        dec, kv_c = inp
        return dec[..., None] * state + kv_c, state

    s0 = jnp.zeros((B, H, K, V), F32)
    _, states = lax.scan(step, s0, (jnp.moveaxis(chunk_decay, 2, 0), jnp.moveaxis(kv, 2, 0)))
    o_inter = jnp.einsum('bhcid,cbhde->bhcie', q_dec, states)
    o = (o_intra + o_inter).transpose(0, 2, 3, 1, 4).reshape(B, S, H, V)
    o = o * lax.rsqrt(jnp.mean(o * o, axis=-1, keepdims=True) + RMS_EPS) * norm_g.astype(F32).reshape(H, V)
    return o.reshape(B, S, H * V).astype(x.dtype) @ w_out

def squared_relu_mlp(x, w_up, w_down):
    return jnp.square(jax.nn.relu(x @ w_up)) @ w_down

def second_inputs(seed: int = 0) -> dict:
    key = jax.random.key(seed)
    ks = jax.random.split(key, 13)
    d_attn_in = N_GROUPS * 3 * ATTN_HEADS * ATTN_HEAD_DIM
    d_attn_out = ATTN_HEADS * ATTN_HEAD_DIM
    d_hgrn_in = 2 * HGRN_HEADS * HGRN_DK + HGRN_HEADS * HGRN_DV
    d_hgrn_out = HGRN_HEADS * HGRN_DV
    nrm = lambda k, shape, scale: jax.random.normal(k, shape, F32) * scale
    return {
        'x': nrm(ks[0], (BATCH, SEQ, D_MODEL), 1.0),
        'attn_w_in': nrm(ks[1], (N_ATTN_LAYERS, D_MODEL, d_attn_in), D_MODEL ** -0.5),
        'attn_w_out': nrm(ks[2], (N_ATTN_LAYERS, d_attn_out, D_MODEL), d_attn_out ** -0.5 * DEEPNORM_BETA),
        'hgrn_w_in': nrm(ks[3], (N_HGRN_LAYERS, D_MODEL, d_hgrn_in), D_MODEL ** -0.5),
        'hgrn_w_out': nrm(ks[4], (N_HGRN_LAYERS, d_hgrn_out, D_MODEL), d_hgrn_out ** -0.5 * DEEPNORM_BETA),
        'hgrn_norm_g': 1.0 + nrm(ks[5], (N_HGRN_LAYERS, d_hgrn_out), 0.02),
        'lb_logits': nrm(ks[6], (DEPTH, HGRN_HEADS * HGRN_DK), 0.1),
        'ln_mix_g': 1.0 + nrm(ks[7], (DEPTH, D_MODEL), 0.02),
        'ln_mix_b': nrm(ks[8], (DEPTH, D_MODEL), 0.02),
        'ln_ffn_g': 1.0 + nrm(ks[9], (DEPTH, D_MODEL), 0.02),
        'ln_ffn_b': nrm(ks[10], (DEPTH, D_MODEL), 0.02),
        'ffn_w_up': nrm(ks[11], (DEPTH, D_MODEL, D_FF), D_MODEL ** -0.5),
        'ffn_w_down': nrm(ks[12], (DEPTH, D_FF, D_MODEL), D_FF ** -0.5 * DEEPNORM_BETA),
    }

def second_block(x, attn_w_in, attn_w_out, hgrn_w_in, hgrn_w_out, hgrn_norm_g, lb_logits,
              ln_mix_g, ln_mix_b, ln_ffn_g, ln_ffn_b, ffn_w_up, ffn_w_down):
    lbs = forget_lower_bounds(lb_logits)
    for i in range(DEPTH):
        j = i // N_MIXERS
        if i % N_MIXERS == 0:
            y = dilated_attention_mixer(x, attn_w_in[j], attn_w_out[j])
        else:
            y = hgrn2_mixer(x, hgrn_w_in[j], hgrn_w_out[j], hgrn_norm_g[j], lbs[i])
        x = layer_norm(DEEPNORM_ALPHA * x + y, ln_mix_g[i], ln_mix_b[i])
        y = squared_relu_mlp(x, ffn_w_up[i], ffn_w_down[i])
        x = layer_norm(DEEPNORM_ALPHA * x + y, ln_ffn_g[i], ln_ffn_b[i])
    return x


def setup_inputs(seed=0):
    out = dict(first_inputs(seed))
    for name, value in second_inputs(seed + 1).items():
        if name != "x":
            out[name + "_2"] = value
    return out


def reference(
    x, c, norm1_g, norm2_g, w_ada, b_ada, ssm_a_re, ssm_a_im, ssm_log_step, ssm_b_re, ssm_b_im,
    ssm_c_re, ssm_c_im, ssm_d, ssm_w_out, conv_w_in, conv_w, conv_w_out, w_ffn_in, w_ffn_out,
    final_g, attn_w_in_2, attn_w_out_2, hgrn_w_in_2, hgrn_w_out_2, hgrn_norm_g_2, lb_logits_2,
    ln_mix_g_2, ln_mix_b_2, ln_ffn_g_2, ln_ffn_b_2, ffn_w_up_2, ffn_w_down_2,
):
    x = first_block(
        x, c, norm1_g, norm2_g, w_ada, b_ada, ssm_a_re, ssm_a_im, ssm_log_step, ssm_b_re,
        ssm_b_im, ssm_c_re, ssm_c_im, ssm_d, ssm_w_out, conv_w_in, conv_w, conv_w_out, w_ffn_in,
        w_ffn_out, final_g,
    )
    return second_block(
        x, attn_w_in_2, attn_w_out_2, hgrn_w_in_2, hgrn_w_out_2, hgrn_norm_g_2, lb_logits_2,
        ln_mix_g_2, ln_mix_b_2, ln_ffn_g_2, ln_ffn_b_2, ffn_w_up_2, ffn_w_down_2,
    )


_drawn_inputs = setup_inputs


def setup_inputs(seed=0):
    import zlib

    import numpy as np

    out = dict(_drawn_inputs(seed))
    spreads = {}
    factors = {'norm1_g': 4.498,
     'norm2_g': 6.319,
     'b_ada': 2.91,
     'ssm_a_re': 64.0,
     'ssm_a_im': 47.384,
     'ssm_log_step': 55.64,
     'ssm_b_re': 64.0,
     'ssm_b_im': 64.0,
     'ssm_c_re': 64.0,
     'ssm_c_im': 64.0,
     'final_g': 2.819,
     'hgrn_norm_g_2': 24.077,
     'lb_logits_2': 8.0}
    for name, (base, spread) in spreads.items():
        noise = np.random.default_rng([zlib.crc32(name.encode()), seed]).standard_normal(out[name].shape)
        drawn = base * np.exp(spread * noise) if base else spread * noise
        out[name] = __import__('jax').numpy.asarray(drawn.astype(out[name].dtype))
    for name, factor in factors.items():
        out[name] = (out[name] * factor).astype(out[name].dtype)
    return out
```

```python
import math
from contextlib import ExitStack

import numpy as np
from concourse import mybir
from concourse.alu_op_type import AluOpType as ALU

F32 = mybir.dt.float32
F32R = mybir.dt.float32r
BF16 = mybir.dt.bfloat16
I32 = mybir.dt.int32
ACT = mybir.ActivationFunctionType
AX = mybir.AxisListType

P = 128
D = 1024
T = 512
KT = D // P
HALF = 4 * 512
FFN0 = 2816
FFN1 = 4096
DFF_CHUNKS0 = (8, 8, 6)
CL = 8
NC_S5 = T // CL
ALPHA = 4 ** 0.25
RMS_EPS, LN_EPS = 1e-6, 1e-5
N_ADA = 24
NEG = -1.0e30

P_SSM = 0
P_FFN_A = P_SSM + 4
P_CONV = P_FFN_A + 17
P_CONVO = P_CONV + 8
P_FFN_B = P_CONVO + 2
P_ATTN = P_FFN_B + 17
P_ATTNO = P_ATTN + 24
P_FFN_C = P_ATTNO + 2
P_HGRN = P_FFN_C + 16
P_HGRNO = P_HGRN + 8
P_FFN_D = P_HGRNO + 2
N_PAIRS = P_FFN_D + 16


def half_width(p):
    if P_CONV <= p < P_CONVO:
        return (4 * 384, 4 * 384)
    if P_ATTN <= p < P_ATTNO:
        return {0: (2048, 2048), 1: (1024, 1024), 2: (1536, 1536)}[(p - P_ATTN) % 3]
    if P_HGRN <= p < P_HGRNO:
        return {0: (2048, 2048), 1: (1024, 1024)}[(p - P_HGRN) % 2]
    if p in (P_FFN_A + 15, P_FFN_A + 16, P_FFN_B + 15, P_FFN_B + 16):
        return (2048, 1024)
    return (2048, 2048)


def build(nc, xT, xU, cT, adaw, bada, norms, s5a, s5bc, s5d, wstream, convw, lnp, hgn, lbl,
          rot, masks, hmask, consts, jsel, gsel, out):
    with ExitStack() as ctx:
        masks = masks.bitcast(BF16)

        def sem(name):
            return ctx.enter_context(nc.semaphore(name))

        def sb(name, shape, dt=F32, c=ctx):
            return c.enter_context(nc.sbuf_tensor(name, shape, dt))

        X = sb("X", [P, KT, T])
        Gh = sb("Gh", [P, KT, T], F32R)
        Gl = sb("Gl", [P, KT, T], F32R)
        raw = sb("raw", [P, 2, HALF])
        cst = sb("cst", [P, 3 * P + 4])
        ident, ones_d, ones_h = cst[:, 0:P], cst[:, P:2 * P], cst[:, 2 * P:3 * P]
        identb = sb("identb", [P, P], BF16)
        MODS = sb("MODS", [P, 96])
        NRM = sb("NRM", [P, 5, KT])
        AM = sb("AM", [P, 4, KT])
        LNP = sb("LNP", [P, 8, KT])
        CW = sb("CW", [P, 3, KT])
        HG = sb("HG", [P, KT])
        bada2 = sb("bada2", [P, 48])
        LB = sb("LB", [P, 4, KT])
        S5D = sb("S5D", [P, KT])
        sq = sb("sq", [P, 2, T])
        Rn = sb("Rn", [P, T])
        PS = ctx.enter_context(nc.psum_tensor("PS", [P, 8, 512], F32))

        s5 = ExitStack()
        XU = sb("XU", [P, 64, NC_S5], c=s5)
        bada_s = sb("bada_s", [P, 48], c=s5)
        c_act = sb("c_act", [P, D], c=s5)
        S5A = sb("S5A", [P, 3, 32], c=s5)
        BC = sb("BC", [P, 4, 32, 16], c=s5)
        GS = sb("GS", [P, 8, P], c=s5)
        JS = sb("JS", [1, 8, P], c=s5)
        BM = sb("BM", [P, 64], c=s5)
        prm = sb("prm", [P, 24, 32], c=s5)
        prmi = sb("prmi", [P, 32], I32, c=s5)
        AP_ = sb("AP_", [P, 2, 9, 32], c=s5)
        QP = sb("QP", [P, 2, 8, 32], c=s5)
        PW = sb("PW", [P, 2, 6, 32], c=s5)
        tw = sb("tw", [P, 2, 32], c=s5)
        CS = sb("CS", [P, 2, 32, NC_S5], c=s5)
        RHO = sb("RHO", [P, 32, NC_S5], c=s5)
        AB_U = sb("AB_U", [P, 8, 16], c=s5)
        AB_f = sb("AB_f", [P, 2, KT], c=s5)
        RU = sb("RU", [P, NC_S5], c=s5)
        Et = sb("Et", [P, 2, 2, 9, 4, 16], c=s5)
        Ft = sb("Ft", [P, 2, 2, 4, 8, 16], c=s5)
        etmp = sb("etmp", [P, 2, 9, 4, 16], c=s5)
        ftmp = sb("ftmp", [P, 2, 4, 8, 16], c=s5)
        Bb = sb("Bb", [P, 2, 2, 64], c=s5)
        FT = sb("FT", [P, 2, 4, P], c=s5)
        Kf = sb("Kf", [P, 8, P], c=s5)
        u_s = sb("u_s", [P, 2, T], c=s5)
        U_s = sb("U_s", [P, 2, 8, NC_S5], c=s5)
        rt = sb("rt", [P, 4, 4 * NC_S5], c=s5)
        ZZ = sb("ZZ", [P, 2, 4 * NC_S5], c=s5)
        WW = sb("WW", [P, 2, 4 * NC_S5], c=s5)
        Xin = sb("Xin", [P, 2, 4, NC_S5 + 1], c=s5)
        Yi = sb("Yi", [64, 8, 8, 16], c=s5)
        yv = sb("yv", [P, T], c=s5)
        yg = sb("yg", [P, T], c=s5)
        s5.close()

        Hh = sb("Hh", [P, KT, T], F32R)
        Hl = sb("Hl", [P, KT, T], F32R)
        Wh = sb("Wh", [P, 2, 2 * HALF], F32R)
        Wl = sb("Wl", [P, 2, 2 * HALF], F32R)
        tmp = sb("tmp", [P, 4, T])
        nv = sb("nv", [P, 3, T])
        mu = sb("mu", [P, T])

        at = ExitStack()
        ROT = tmp[:, 2:4, :]
        MK0 = sb("MK0", [P, 4, 512], BF16, c=at)
        MK1 = sb("MK1", [P, 256], BF16, c=at)
        QK = sb("QK", [P, 6, T], c=at)
        V = sb("V", [P, 4, 3 * P], c=at)
        swp = mu
        Pr = nv[:, :, :].rearrange("p a t -> p (a t)")[:, 0:768]
        PT = nv[:, :, :].rearrange("p a t -> p (a t)")[:, 768:1536]
        sm = sb("sm", [P, 2, 4], c=at)
        at.close()

        hg = ExitStack()
        HM = sb("HM", [P, 4, P], c=hg)
        RST = sb("RST", [P, T], c=hg)
        HQ, HKD, HKE, HS0, HS1 = (sb(n, [P, T], c=hg) for n in ("HQ", "HKD", "HKE", "HS0", "HS1"))
        Hq = (HQ, sq[:, 1, :])
        Hkd = (HKD, tmp[:, 1, :])
        Hke = (HKE, tmp[:, 2, :])
        Hf = (HS1, nv[:, 0, :])
        Hb = (HS0, tmp[:, 0, :])
        Heb = (tmp[:, 3, :], nv[:, 2, :])
        Hemb = (mu, nv[:, 1, :])
        HkT = (HS0, mu)
        Ham = (HS1, tmp[:, 0, :])
        Hv = (nv[:, 0, :], nv[:, 2, :])
        Hln = (nv[:, 1, :], HS0)
        Hr = (Rn, HS1)
        Hon = tmp[:, 3, :]
        HV = sb("HV", [P, 4, 256], c=hg)
        SS = sb("SS", [P, 7, P], c=hg)
        hg.close()
        cv = ExitStack()
        CVb = sb("CVb", [P, 2 + T], c=cv)
        adab = sb("adab", [P, 2, HALF], c=cv)
        c_act2 = sb("c_act2", [P, D], c=cv)
        cv.close()

        consts_in = sem("consts_in")
        x_in = sem("x_in")
        xu_in = sem("xu_in")
        late_in = sem("late_in")
        raw_in = [sem("raw_in0"), sem("raw_in1")]
        ada_used = sem("ada_used")
        ada2_in = [sem("ada2_in0"), sem("ada2_in1")]
        ada2_used, c2_in, c2_act = sem("ada2_used"), sem("c2_in"), sem("c2_act")
        split_h = sem("split_h")
        split_l = sem("split_l")
        acc_ready = sem("acc_ready")
        free_act = sem("free_act")
        free_dve = sem("free_dve")
        out_done = sem("out_done")
        v_ord = sem("v_ord")
        a_ord = sem("a_ord")

        nm_x = sem("nm_x")
        nm_sq = sem("nm_sq")
        nm_mm = sem("nm_mm")
        nm_xs = sem("nm_xs")
        nm_mean = sem("nm_mean")
        nm_v = sem("nm_v")
        nm_r0 = sem("nm_r0")
        nm_t = sem("nm_t")
        nm_h = sem("nm_h")
        nm_l = sem("nm_l")

        class Order:
            def __init__(self, eng, s):
                self.eng, self.s, self.n = eng, s, 0

            def step(self, ins):
                ins.then_inc(self.s, 1)
                self.n += 1

            def sync(self):
                self.eng.wait_ge(self.s, self.n)

            def link(self, ins):
                self.step(ins)
                self.sync()

        s5_s = {n: sem("s5_" + n) for n in (
            "fir", "mods", "cact", "ab", "sel", "rn", "ru", "abu", "tab", "e", "f", "tr", "ftc", "kx", "kf", "inc",
            "xin", "inter", "yi", "y", "yv", "g", "gh", "gl", "u", "prm_a", "prm_v")}
        lb_diff, lb_done = sem("lb_diff"), sem("lb_done")
        hid_t = sem("hid_t")
        hid_f = sem("hid_f")
        hid_h = sem("hid_h")
        hid_l = sem("hid_l")
        at_s = {n: sem("at_" + n) for n in ("swap", "swf", "qk", "v", "s", "max", "p", "pn", "pt", "ptc", "o", "otl")}
        hg_s = {n: sem("hg_" + n) for n in (
            "sf",
            "f",
            "k1",
            "ln",
            "b",
            "bd",
            "ex",
            "sg",
            "qd",
            "ke",
            "v",
            "a",
            "kt",
            "ktc",
            "kv",
            "am",
            "st",
            "o",
            "sq",
            "oc",
            "ms",
            "v2",
            "r0",
            "on",
            "gh",
            "gl")}

        block = ctx.enter_context(nc.Block())

        HID = {"A": 0, "CV": 22, "B": 30, "C": 52, "D": 84}

        @block.sync
        def _(sp):
            for dst, src in ((cst[:, 0:3 * P], consts[:, :]), (c_act[:, :], cT), (S5A[:, :, :], s5a), (BC[:, :, :, :], s5bc),
                             (BM[:, :], hmask[:, 4 * P + T:4 * P + T + 64]), (NRM[:, :, :], norms),
                             (bada_s[:, :], bada[:, 0:48]), (S5D[:, :], s5d), (GS[:, :, :], gsel), (JS[:, :, :], jsel)):
                sp.dma_start(dst, src).then_inc(consts_in, 16)
            sp.dma_start(X[:, :, :], xT).then_inc(x_in, 16)
            for a in range(2):
                sp.dma_start(raw[:, a, :], adaw[a]).then_inc(raw_in[a], 16)
            sp.dma_start(XU[:, :, :], xU).then_inc(xu_in, 16)
            for a in range(2, N_ADA):
                sp.wait_ge(ada_used, a - 1)
                sp.dma_start(raw[:, a % 2, :], adaw[a]).then_inc(raw_in[a % 2], 16)
            for dst, src in ((LNP[:, :, :], lnp), (CW[:, :, :], convw), (HG[:, :], hgn), (LB[:, 0:2, :], lbl), (bada2[:, :], bada[:, 48:96])):
                sp.dma_start(dst, src).then_inc(late_in, 16)

            def load(p, widths):
                for h in range(2):
                    if isinstance(p, int) and p == 0:
                        sp.wait_ge(ada_used, N_ADA - 1 + h)
                    else:
                        sp.wait_ge(split_l, 2 * p - 1 + h)
                    sp.dma_start(raw[:, h, 0:widths[h]], wstream[p][:, h * HALF:h * HALF + widths[h]]).then_inc(raw_in[h], 16)

            def load_run(first, end):
                with sp.Fori(0, end - first) as i:
                    load(first + i, half_width(first))

            def load_swiglu(first):
                load_run(first, first + 15)
                load(first + 15, half_width(first + 15))
                load(first + 16, half_width(first + 16))

            load(0, half_width(0))
            load_run(1, P_FFN_A)
            load_swiglu(P_FFN_A)
            load_run(P_CONV, P_CONVO)
            load_run(P_CONVO, P_FFN_B)
            load_swiglu(P_FFN_B)
            load(P_ATTN, half_width(P_ATTN))
            load(P_ATTN + 1, half_width(P_ATTN + 1))
            sp.wait_ge(nm_x, 8 * 4)
            for dst, src in ((ROT[:, :, :], rot[:, :, :]), (MK0[:, :, :], masks[:, 0:4 * 512].rearrange("p (r k) -> p r k", r=4)),
                             (MK1[:, :], masks[:, 4 * 512:4 * 512 + 256]), (identb[:, :], masks[:, 4 * 512 + 256:4 * 512 + 384])):
                sp.dma_start(dst, src).then_inc(late_in, 16)
            load(P_ATTN + 2, half_width(P_ATTN + 2))
            with sp.Fori(0, 7) as i:
                for q in range(3):
                    load(P_ATTN + 3 + 3 * i + q, half_width(P_ATTN + q))
            load_run(P_ATTNO, P_HGRN)
            load(P_HGRN, half_width(P_HGRN))
            load(P_HGRN + 1, half_width(P_HGRN + 1))
            sp.wait_ge(nm_x, 8 * 6)
            for dst, src in ((HM[:, :, :], hmask[:, 0:4 * P].rearrange("p (r k) -> p r k", r=4)), (RST[:, :], hmask[:, 4 * P:4 * P + T])):
                sp.dma_start(dst, src).then_inc(late_in, 16)
            with sp.Fori(0, 3) as i:
                for q in range(2):
                    load(P_HGRN + 2 + 2 * i + q, half_width(P_HGRN + q))
            load_run(P_HGRNO, N_PAIRS)
            sp.wait_ge(nm_l, 8 * 8)
            sp.dma_start(out, X[:, :, :]).then_inc(out_done, 16)
            sp.wait_ge(out_done, 16)

        @block.tensor
        def _(pe):
            mm = nc.tensor.matmul

            def norm_sums(n, bank, ln, ks=None):
                for k in range(KT) if ks is None else ks:
                    pe.wait_ge(nm_sq, 8 * n + k + 1)
                    mm(PS[:, bank, :], ones_d, sq[:, k % 2, :], start=k == 0, stop=k == KT - 1).then_inc(nm_mm, 1)
                if ln is not None:
                    pe.wait_ge(nm_xs, ln + 1)
                    mm(PS[:, bank + 1, :], ones_d, nv[:, 0, :], start=True, stop=True).then_inc(nm_mean, 1)

            pe.wait_ge(consts_in, 160)
            norm_sums(0, 7, None)
            pe.wait_ge(s5_s["ab"], 1)
            for g8 in range(8):
                last = mm(PS[:, 1, 16 * g8:16 * g8 + 16], GS[:, g8, :], AB_f[:, :, :].rearrange("p a t -> p (a t)"), start=True, stop=True)
            last.then_inc(s5_s["sel"], 1)
            pe.wait_ge(s5_s["rn"], 1)
            rr = Rn[0:1, :].rearrange("p (c j) -> p j c", j=CL)
            for j in range(CL):
                last = mm(PS[:, 2, 0:NC_S5], JS[:, j, :], rr[:, j, :], start=j == 0, stop=j == CL - 1)
            last.then_inc(s5_s["ru"], 1)
            pe.wait_ge(s5_s["abu"], 1)

            def s5_lags(t):
                b = t % 2
                pe.wait_ge(s5_s["f"], t + 1)
                if t:
                    pe.wait_ge(s5_s["ftc"], t)
                for c in range(2):
                    for i in range(4):
                        last = nc.tensor.transpose(PS[:, 1 + c, i * P:(i + 1) * P], Ft[:, b, c, i, :, :].rearrange("p j h -> p (j h)"), ident)
                last.then_inc(s5_s["tr"], 1)
                pe.wait_ge(s5_s["e"], t + 1)
                if t:
                    pe.wait_ge(s5_s["kf"], t)
                for e in range(2):
                    r = slice(64 * e, 64 * e + 64)
                    for c in range(2):
                        last = mm(PS[r, 3, :], Bb[r, b, c, :], Et[r, b, c, 0:8, :, :].rearrange("p l i h -> p (l i h)"),
                                  start=c == 0, stop=c == 1)
                last.then_inc(s5_s["kx"], 1)

            def s5_increments(t):
                b = t % 2
                pe.wait_ge(s5_s["ftc"], t + 1)
                pe.wait_ge(s5_s["u"], t + 1)
                if t:
                    pe.wait_ge(s5_s["xin"], t)
                for i in range(4):
                    for e in range(2):
                        for c in range(2):
                            last = mm(PS[64 * e:64 * e + 64, 4, c * 256 + i * 64:c * 256 + i * 64 + 64],
                                      FT[:, c, i, 64 * e:64 * e + 64], U_s[:, b, 4 * e + i, :], start=True, stop=True)
                last.then_inc(s5_s["inc"], 1)

            s5_lags(0)
            s5_increments(0)
            for t in range(KT):
                b = t % 2
                pe.wait_ge(s5_s["kf"], t + 1)
                if t:
                    pe.wait_ge(s5_s["yv"], t)
                yp = PS[:, 7, :].rearrange("p (c j) -> p c j", j=CL)
                uv = u_s[:, b, :].rearrange("p (c j) -> p c j", j=CL)
                for l in range(CL):
                    last = mm(yp[:, :, l:CL], Kf[:, l, :], uv[:, :, 0:CL - l], start=l == 0, stop=False, skip_group_check=True)
                last.then_inc(s5_s["fir"], 1)
                if t + 1 < KT:
                    s5_lags(t + 1)
                pe.wait_ge(s5_s["xin"], t + 1)
                if t:
                    pe.wait_ge(s5_s["yi"], t)
                for g in range(8):
                    e, i = g // 4, g % 4
                    r = slice(64 * e, 64 * e + 64)
                    for c in range(2):
                        last = mm(PS[0:64, 5 + g // 4, (g % 4) * P:(g % 4) * P + P], Xin[r, c, i, 0:NC_S5],
                                  Et[r, b, c, 1:9, i, :], start=c == 0, stop=c == 1)
                last.then_inc(s5_s["inter"], 1)
                if t + 1 < KT:
                    s5_increments(t + 1)
                pe.wait_ge(s5_s["yi"], t + 1)
                for j in range(CL):
                    last = mm(yp[:, :, j], Yi[:, j, :, :].rearrange("p g h -> p (g h)"), ident[0:64, 0:64], start=False, stop=j == CL - 1, skip_group_check=True)
                last.then_inc(s5_s["y"], 1)

            def wait_pair(p):
                pe.wait_ge(split_l, 2 * p + 2)
                if not isinstance(p, int) or p >= 2:
                    pe.wait_ge(free_act, p - 1)
                    pe.wait_ge(free_dve, p - 1)

            def product(p, s, kt, nt, xh, xl, by_k=False, ready=None, between=None, lead=4):
                wait_pair(p)
                w = nt * P

                def one(k, m):
                    if ready is not None and m == 0:
                        ready(k)
                    c0 = (k // 4) * HALF + (k % 4) * w + m * P
                    o = PS[:, 4 * s + m, :]
                    mm(o, Wh[:, s, c0:c0 + P], xl[:, k, :], start=k == 0, stop=False)
                    mm(o, Wl[:, s, c0:c0 + P], xh[:, k, :], start=False, stop=False)
                    last = mm(o, Wh[:, s, c0:c0 + P], xh[:, k, :], start=False, stop=k == kt - 1)
                    if k == kt - 1:
                        last.then_inc(acc_ready, 1 if m < nt - 1 else 5 - nt)
                if by_k:
                    for k in range(lead):
                        for m in range(nt):
                            one(k, m)
                    for m in range(nt):
                        for k in range(lead, kt):
                            one(k, m)
                else:
                    for m in range(nt):
                        for k in range(kt):
                            one(k, m)
                        if between is not None:
                            between(m)

            def after_norm(n):
                return lambda k: pe.wait_ge(nm_l, 8 * (n - 1) + k + 1)

            def after_hidden(first):
                return lambda k: pe.wait_ge(hid_l, first + k + 1)

            def swiglu(p0, n, name):
                h0 = HID[name]
                p, done = p0, 0
                for ci, tiles in enumerate(DFF_CHUNKS0):
                    for j in range(tiles // 2):
                        first = ci == 0 and j == 0
                        product(p, p % 2, KT, 4, Hh, Hl, by_k=first, ready=after_norm(n) if first else None)
                        p += 1
                    for d in range(2):
                        if d == 1 and ci == 2:
                            last_product(p, n + 1, tiles, DOWN)
                        else:
                            product(p, p % 2, tiles, 4, Gh, Gl, by_k=d == 0, ready=after_hidden(h0 + done) if d == 0 else None)
                        p += 1
                    done += tiles

            def sq_relu(p0, n, name, ln):
                h0 = HID[name]
                for ci in range(4):
                    for j in range(4):
                        p = p0 + 4 * ci + j
                        first = ci == 0 and j == 0
                        if j < 2:
                            product(p, j % 2, KT, 4, Hh, Hl, by_k=first, ready=after_norm(n) if first else None, lead=6)
                        elif j == 3 and ci == 3:
                            last_product(p, n + 1, KT, DOWN, ln)
                        else:
                            product(p, j % 2, KT, 4, Gh, Gl, by_k=j == 2, ready=after_hidden(h0 + 8 * ci) if j == 2 else None)

            def last_product(p, n, kt, done, ln=None):
                bank = 4 * ((p + 1) % 2)

                def sums(m):
                    if m == 1:
                        pe.wait_ge(free_act, p)
                        pe.wait_ge(free_dve, p)
                    if m in done:
                        norm_sums(n, bank, None, done[m])
                product(p, p % 2, kt, 4, Gh, Gl, between=sums)
                norm_sums(n, bank, ln, range(max(max(r) for r in done.values()) + 1, KT))

            DOWN = {1: range(0, 2), 2: range(2, 4), 3: range(4, 6)}

            for j in range(3):
                product(P_SSM + j, j % 2, KT, 4, Gh, Gl, by_k=j == 0,
                        ready=(lambda k: pe.wait_ge(s5_s["gl"], k + 1)) if j == 0 else None)
            last_product(P_SSM + 3, 1, KT, {3: range(0, 6)})
            swiglu(P_FFN_A, 1, "A")
            for j in range(8):
                product(P_CONV + j, (P_CONV + j) % 2, KT, 3, Hh, Hl, by_k=j == 0, ready=after_norm(2) if j == 0 else None)
            product(P_CONVO, P_CONVO % 2, KT, 4, Gh, Gl, by_k=True, ready=after_hidden(HID["CV"]))
            last_product(P_CONVO + 1, 3, KT, DOWN)
            swiglu(P_FFN_B, 3, "B")

            def tokens(x, k, r, perm):
                return x[:, k, r * P:(r + 1) * P] if not perm else x[:, k, :].rearrange("p (n r) -> p r n", r=4)[:, r, :]

            pe.wait_ge(late_in, 16 * 9)
            for un in range(8):
                p = P_ATTN + 3 * un
                product(p, p % 2, KT, 4, Hh, Hl, by_k=un == 0, ready=after_norm(4) if un == 0 else None)
                if un:
                    pe.wait_ge(at_s["otl"], 2 * un)
                product(p + 1, (p + 1) % 2, KT, 2, Hh, Hl)
                p2 = p + 2
                s = p2 % 2
                wait_pair(p2)
                for r in range(4):
                    for perm, n0, n1 in ((False, 0, P), (True, P, 3 * P)):
                        for k in range(KT):
                            c0 = (k // 4) * HALF + (k % 4) * 384
                            o = PS[:, 4 * s + r, n0:n1]
                            mm(o, tokens(Hl, k, r, perm), Wh[:, s, c0 + n0:c0 + n1], start=k == 0, stop=False)
                            mm(o, tokens(Hh, k, r, perm), Wl[:, s, c0 + n0:c0 + n1], start=False, stop=False)
                            last = mm(o, tokens(Hh, k, r, perm), Wh[:, s, c0 + n0:c0 + n1], start=False, stop=k == KT - 1)
                    last.then_inc(acc_ready, 1)
                sb0, tb0 = 4 * (1 - s), 4 * s
                pe.wait_ge(free_act, p2)
                pe.wait_ge(free_dve, p2)
                pe.wait_ge(at_s["qk"], 6 * (un + 1))

                def scores(g):
                    h, r = g // 4, g % 4
                    b = sb0 + 2 * (g % 2)
                    rows = slice(64 * h, 64 * h + 64)
                    q = [QK[rows, 2 * x, :].rearrange("p (n r) -> p r n", r=4)[:, r, :] for x in range(3)]
                    k = [QK[rows, 2 * x + 1, :].rearrange("p (n r) -> p r n", r=4)[:, r, :] for x in range(3)]
                    tot = 8 * un + g
                    if g >= 2:
                        pe.wait_ge(at_s["p"], tot - 1)
                    mm(PS[:, b, :], identb[:, :], MK0[:, r, :], start=True, stop=False)
                    mm(PS[:, b, :], q[0], QK[rows, 1, :], start=False, stop=True)
                    mm(PS[:, b + 1, 0:256], identb[:, :], MK1[:, :], start=True, stop=False, skip_group_check=True)
                    mm(PS[:, b + 1, 0:P], q[1], k[1], start=False, stop=False, skip_group_check=True)
                    mm(PS[:, b + 1, P:2 * P], q[2], k[2], start=False, stop=True, skip_group_check=True).then_inc(at_s["s"], 1)

                scores(0)

                def outputs(g):
                    tot = 8 * un + g
                    h, r = g // 4, g % 4
                    pe.wait_ge(at_s["ptc"], tot + 1)
                    for j in range(6):
                        v = V[:, j, 64 * h:64 * h + 64] if j < 4 else V[:, r, (j - 3) * P + 64 * h:(j - 3) * P + 64 * h + 64]
                        last = mm(PS[64 * h:64 * h + 64, tb0 + 2 + h, r * P:(r + 1) * P], v, PT[:, j * P:(j + 1) * P], start=j == 0, stop=j == 5)
                    last.then_inc(at_s["o"], 1)

                for g in range(8):
                    if g < 7:
                        scores(g + 1)
                    if g:
                        outputs(g - 1)
                    tot = 8 * un + g
                    pe.wait_ge(at_s["pn"], tot + 1)
                    if g == 0:
                        pe.wait_ge(at_s["v"], un + 1)
                    if g == 0 and un:
                        pe.wait_ge(at_s["ptc"], tot)
                    for j in range(6):
                        last = nc.tensor.transpose(PS[:, tb0 + j // 4, (j % 4) * P:(j % 4) * P + P], Pr[:, j * P:(j + 1) * P], ident)
                    last.then_inc(at_s["pt"], 1)
                outputs(7)

            product(P_ATTNO, P_ATTNO % 2, KT, 4, Gh, Gl, by_k=True, ready=lambda k: pe.wait_ge(at_s["otl"], 2 * (k + 1)))
            last_product(P_ATTNO + 1, 5, KT, DOWN, 0)
            sq_relu(P_FFN_C, 5, "C", 1)

            pe.wait_ge(late_in, 16 * 11)
            for un in range(4):
                p = P_HGRN + 2 * un
                product(p, 0, KT, 4, Hh, Hl, by_k=un == 0, ready=after_norm(6) if un == 0 else None, lead=6)
                wait_pair(p + 1)
                for r in range(4):
                    for k in range(KT):
                        c0 = (k // 4) * HALF + (k % 4) * 256
                        o = PS[:, 4 + r, 0:256]
                        tk = slice(r * P, (r + 1) * P)
                        mm(o, Hl[:, k, tk], Wh[:, 1, c0:c0 + 256], start=k == 0, stop=False)
                        mm(o, Hh[:, k, tk], Wl[:, 1, c0:c0 + 256], start=False, stop=False)
                        last = mm(o, Hh[:, k, tk], Wh[:, 1, c0:c0 + 256], start=False, stop=k == KT - 1)
                    last.then_inc(acc_ready, 1)
                for h in range(2):
                    g = 2 * un + h
                    if h == 0:
                        pe.wait_ge(hg_s["ke"], 2 * un + 2)
                    else:
                        pe.wait_ge(hg_s["v"], un + 1)
                    for r in range(4):
                        last = nc.tensor.transpose(PS[:, 4 * h + 1, r * P:(r + 1) * P], Hke[h][:, r * P:(r + 1) * P], ident)
                    last.then_inc(hg_s["kt"], 1)
                    for r in range(4):
                        last = mm(PS[:, 4 * h, r * P:(r + 1) * P], Hkd[h][:, r * P:(r + 1) * P], Hq[h][:, r * P:(r + 1) * P], start=True, stop=True)
                    last.then_inc(hg_s["a"], 1)
                for h in range(2):
                    g = 2 * un + h
                    vh = HV[:, :, h * P:(h + 1) * P]
                    pe.wait_ge(hg_s["ktc"], g + 1)
                    kT = HkT[h][:, :].rearrange("p (r d) -> p r d", r=4)
                    for c in range(7):
                        rows = slice(64 * (c % 2), 64 * (c % 2) + 64)
                        last = mm(PS[:, 4 * h + 2 + c % 2, (c // 2) * P:(c // 2) * P + P], kT[rows, c // 2, :], vh[rows, c // 2, :], start=True, stop=True)
                    last.then_inc(hg_s["kv"], 1)
                for h in range(2):
                    g = 2 * un + h
                    vh = HV[:, :, h * P:(h + 1) * P]
                    pe.wait_ge(hg_s["am"], g + 1)
                    pe.wait_ge(hg_s["st"], g + 1)
                    am = Ham[h][:, :].rearrange("p (r i) -> p r i", r=4)
                    for r in range(4):
                        mm(PS[:, 4 * h, r * P:(r + 1) * P], vh[:, r, :], am[:, r, :], start=True, stop=False, skip_group_check=True)
                        for c in (2 * r, 2 * r + 1):
                            if c:
                                last = mm(PS[:, 4 * h, c * 64:c * 64 + 64], SS[:, c - 1, :], Hq[h][:, c * 64:c * 64 + 64],
                                          start=False, stop=c % 2 == 1, skip_group_check=True)
                    last.then_inc(hg_s["o"], 1)
                    if h == 0:
                        pe.wait_ge(hg_s["sq"], g + 1)
                        mm(PS[:, 1, :], ones_h, sq[:, 0, :], start=True, stop=True).then_inc(hg_s["ms"], 1)
                pe.wait_ge(hg_s["sq"], 2 * un + 2)
                mm(PS[:, 5, :], ones_h, sq[:, 1, :], start=True, stop=True).then_inc(hg_s["ms"], 1)
            product(P_HGRNO, P_HGRNO % 2, KT, 4, Gh, Gl, by_k=True, ready=lambda k: pe.wait_ge(hg_s["gl"], k + 1))
            last_product(P_HGRNO + 1, 7, KT, DOWN, 2)
            sq_relu(P_FFN_D, 7, "D", 3)

        @block.scalar
        def _(act):
            o = Order(act, a_ord)
            A = nc.scalar.activation

            def squares(n):
                for k in range(KT):
                    if n:
                        act.wait_ge(nm_x, 8 * (n - 1) + k + 1)
                    if 8 * n + k >= 2:
                        act.wait_ge(nm_mm, 8 * n + k - 1)
                    A(sq[:, k % 2, :], X[:, k, :], ACT.Square).then_inc(nm_sq, 1)

            def rsqrt_estimate(n):
                act.wait_ge(nm_v, n + 1)
                o.link(A(nv[:, 1, :], nv[:, 2, :], ACT.Ln))
                A(Rn[:, :], nv[:, 1, :], ACT.Exp, scale=-0.5).then_inc(nm_r0, 1)

            def split(p, widths):
                s = p % 2
                for h in range(2):
                    act.wait_ge(raw_in[h], 16 * (N_ADA // 2 + p + 1))
                    if h == 0 and p >= 2:
                        act.wait_ge(acc_ready, 4 * (p - 1))
                    nc.scalar.copy(Wh[:, s, h * HALF:h * HALF + widths[h]], raw[:, h, 0:widths[h]]).then_inc(split_h, 1)

            def ahead(p):
                if p + 1 < N_PAIRS:
                    split(p + 1, half_width(p + 1))

            def norm(n, shift=None):
                squares(n)
                if n == 2:
                    act.wait_ge(s5_s["mods"], 2)
                rsqrt_estimate(n)
                for k in range(KT):
                    act.wait_ge(nm_t, 8 * (n - 1) + k + 1)
                    if shift is None:
                        nc.scalar.copy(Hh[:, k, :], X[:, k, :]).then_inc(nm_h, 1)
                    else:
                        A(Hh[:, k, :], tmp[:, k % 4, :], ACT.Identity, bias=shift(k)).then_inc(nm_h, 1)

            act.wait_ge(consts_in, 160)
            A(c_act[:, :], c_act[:, :], ACT.Silu).then_inc(s5_s["cact"], 1)
            act.wait_ge(s5_s["prm_v"], 1)
            A(prm[:, 10, :], prm[:, 9, :], ACT.Sin).then_inc(s5_s["prm_a"], 1)
            A(prm[:, 11, :], prm[:, 9, :], ACT.Sin, scale=0.5).then_inc(s5_s["prm_a"], 1)
            act.wait_ge(x_in, 16)
            squares(0)
            act.wait_ge(nm_v, 1)
            o.link(A(yv[:, :], yg[:, :], ACT.Ln))
            A(u_s[:, 0, :], yv[:, :], ACT.Exp, scale=-0.5).then_inc(nm_r0, 1)
            def s5_ft(t):
                act.wait_ge(s5_s["tr"], t + 1)
                if t:
                    act.wait_ge(s5_s["inc"], t)
                nc.scalar.copy(FT[:, :, :, :].rearrange("p c i s -> p (c i s)"), PS[:, 1:3, :].rearrange("p b n -> p (b n)")).then_inc(s5_s["ftc"], 1)

            s5_ft(0)
            for t in range(KT):
                if t + 1 < KT:
                    s5_ft(t + 1)
                act.wait_ge(s5_s["inter"], t + 1)
                if t:
                    act.wait_ge(s5_s["y"], t)
                nc.scalar.copy(Yi[:, :, :, :].rearrange("p j g h -> p g j h"),
                               PS[0:64, 5:7, :].rearrange("p b (g j h) -> p (b g) j h", g=4, j=8)).then_inc(s5_s["yi"], 1)
                act.wait_ge(s5_s["yv"], t + 1)
                if t:
                    act.wait_ge(s5_s["gl"], t)
                o.link(A(yg[:, :], yv[:, :], ACT.Gelu_apprx_tanh))
                nc.scalar.copy(Gh[:, t, :], yg[:, :]).then_inc(s5_s["gh"], 1)

            act.wait_ge(s5_s["gl"], KT)
            act.wait_ge(s5_s["y"], KT)
            act.wait_ge(s5_s["mods"], 1)
            split(0, half_width(0))
            for j in range(4):
                p = P_SSM + j
                ahead(p)
                for m in range(2):
                    if j:
                        act.wait_ge(hid_f, 2 * (j - 1) + m + 1)
                    act.wait_ge(acc_ready, 4 * p + 3 + m)
                    A(tmp[:, m, :], PS[:, 4 * (p % 2) + 2 + m, :], ACT.Sigmoid).then_inc(hid_t, 1)
                act.wait_ge(hid_t, 2 * j + 2)
                act.sem_inc(free_act, 1)
            norm(1, lambda k: MODS[:, 24 + k:25 + k])

            hc = [8, 0]

            def act_free(n_hid_t):
                act.wait_ge(hid_t, n_hid_t)
                act.sem_inc(free_act, 1)

            def up_pair(p, func, g0, nt):
                ahead(p)
                for m in range(nt):
                    t = hc[1] + m
                    act.wait_ge(acc_ready, 4 * p + m + 1)
                    if t >= 4:
                        act.wait_ge(hid_l, t - 3)
                    A(tmp[:, t % 4, :], PS[:, 4 * (p % 2) + m, :], func).then_inc(hid_t, 1)
                hc[0] += nt
                act_free(hc[0])
                for m in range(nt):
                    t = hc[1] + m
                    act.wait_ge(hid_f, 8 + t + 1)
                    nc.scalar.copy(Gh[:, g0 + m, :], tmp[:, t % 4, :]).then_inc(hid_h, 1)
                hc[1] += nt

            def down_pair(p):
                ahead(p)
                act.sem_inc(free_act, 1)

            def swiglu(p0):
                p = p0
                for tiles in DFF_CHUNKS0:
                    for j in range(tiles // 2):
                        up_pair(p, ACT.Silu, 2 * j, 2)
                        p += 1
                    for _ in range(2):
                        down_pair(p)
                        p += 1

            act.wait_ge(c2_in, 16)
            A(c_act2[:, :], c_act2[:, :], ACT.Silu).then_inc(c2_act, 1)
            swiglu(P_FFN_A)
            norm(2, lambda k: MODS[:, 48 + k:49 + k])
            act.wait_ge(lb_diff, 1)
            o.link(A(LB[:, 3, :], LB[:, 2, :], ACT.Sigmoid, scale=-1.0))
            A(LB[:, 2, :], LB[:, 2, :], ACT.Sigmoid).then_inc(lb_done, 1)
            for j in range(8):
                p = P_CONV + j
                t = hc[1]
                ahead(p)
                act.wait_ge(acc_ready, 4 * p + 2)
                act.wait_ge(hid_l, t)
                A(tmp[:, 2, :], PS[:, 4 * (p % 2) + 1, :], ACT.Identity).then_inc(hid_t, 1)
                hc[0] += 1
                act_free(hc[0])
                act.wait_ge(hid_f, 8 + t + 1)
                nc.scalar.copy(Gh[:, j, :], tmp[:, 3, :]).then_inc(hid_h, 1)
                hc[1] += 1
            for j in range(2):
                down_pair(P_CONVO + j)
            norm(3, lambda k: MODS[:, 72 + k:73 + k])
            swiglu(P_FFN_B)
            norm(4)

            nsw = 0
            for un in range(8):
                p = P_ATTN + 3 * un
                for q in range(3):
                    ahead(p + q)
                    s = (p + q) % 2
                    if q == 2:
                        act.wait_ge(acc_ready, 4 * (p + 3))
                        nc.scalar.copy(V[:, :, :], PS[:, 4 * s:4 * s + 4, 0:3 * P]).then_inc(at_s["v"], 1)
                        act.wait_ge(at_s["v"], un + 1)
                        act.sem_inc(free_act, 1)
                        continue
                    for m in range((4, 2)[q]):
                        act.wait_ge(acc_ready, 4 * (p + q) + m + 1)
                        if nsw:
                            act.wait_ge(at_s["swf"], nsw)
                        nsw += 1
                        for a in range(4):
                            ins = nc.scalar.copy(swp[32 * a:32 * a + 32, :], PS[32 * (a ^ 1):32 * (a ^ 1) + 32, 4 * s + m, :])
                        ins.then_inc(at_s["swap"], 1)
                    act.wait_ge(at_s["swap"], nsw)
                    act.sem_inc(free_act, 1)
                for g in range(8):
                    tot = 8 * un + g
                    act.wait_ge(at_s["max"], tot + 1)
                    if tot:
                        act.wait_ge(at_s["pt"], tot)
                    b = 4 * (1 - (p + 2) % 2) + 2 * (g % 2)
                    A(Pr[:, :], PS[:, b:b + 2, :].rearrange("p b n -> p (b n)")[:, 0:768], ACT.Exp, bias=sm[:, 0, g % 4:g % 4 + 1],
                      scale=0.125, accum_out=sm[:, 1, g % 4:g % 4 + 1]).then_inc(at_s["p"], 1)
                    act.wait_ge(at_s["pt"], tot + 1)
                    if tot:
                        act.wait_ge(at_s["o"], tot)
                    nc.scalar.copy(PT[:, :], PS[:, 4 * ((p + 2) % 2):4 * ((p + 2) % 2) + 2, :].rearrange("p b n -> p (b n)")[:, 0:768]).then_inc(at_s["ptc"], 1)
            for j in range(2):
                down_pair(P_ATTNO + j)
            norm(5, lambda k: LNP[:, 1, k:k + 1])

            def sq_relu(p0):
                for ci in range(4):
                    for j in range(4):
                        p = p0 + 4 * ci + j
                        if j < 2:
                            up_pair(p, ACT.Relu, 4 * j, 4)
                        else:
                            down_pair(p)

            sq_relu(P_FFN_C)
            norm(6, lambda k: LNP[:, 3, k:k + 1])

            for un in range(4):
                p = P_HGRN + 2 * un
                ahead(p)
                if un:
                    act.wait_ge(hg_s["gl"], 2 * un)
                for h in range(2):
                    act.wait_ge(acc_ready, 4 * p + 1 + h)
                    A(Hf[h][:, :], PS[:, h, :], ACT.Sigmoid).then_inc(hg_s["sf"], 1)
                    A(Hemb[h][:, :], PS[:, h, :], ACT.Sigmoid, scale=-1.0).then_inc(hg_s["sf"], 1)
                for h in range(2):
                    act.wait_ge(hg_s["f"], 2 * un + h + 1)
                    A(Hf[h][:, :], Hf[h][:, :], ACT.Ln).then_inc(hg_s["ln"], 1)
                for h in range(2):
                    g = 2 * un + h
                    act.wait_ge(hg_s["b"], g + 1)
                    A(Heb[h][:, :], Hb[h][:, :], ACT.Exp).then_inc(hg_s["ex"], 1)
                    act.wait_ge(hg_s["k1"], g + 1)
                    A(Hemb[h][:, :], Hb[h][:, :], ACT.Exp, scale=-1.0).then_inc(hg_s["ex"], 1)
                    act.wait_ge(hg_s["bd"], g + 1)
                    A(Hf[h][:, :], Hf[h][:, :], ACT.Exp).then_inc(hg_s["ex"], 1)
                act.wait_ge(hg_s["ex"], 6 * un + 6)
                for h in range(2):
                    act.wait_ge(acc_ready, 4 * p + 3 + h)
                    A(Hb[h][:, :], PS[:, 2 + h, :], ACT.Sigmoid).then_inc(hg_s["sg"], 1)
                ahead(p + 1)
                act.wait_ge(acc_ready, 4 * (p + 2))
                nc.scalar.copy(HV[:, :, :], PS[:, 4:8, 0:256]).then_inc(hg_s["v"], 1)
                for h in range(2):
                    g = 2 * un + h
                    act.wait_ge(hg_s["ke"], g + 1)
                    act.wait_ge(hg_s["kt"], g + 1)
                    nc.scalar.copy(HkT[h][:, :], PS[:, 4 * h + 1, :]).then_inc(hg_s["ktc"], 1)
                for h in range(2):
                    g = 2 * un + h
                    act.wait_ge(hg_s["o"], g + 1)
                    A(sq[:, h, :], PS[:, 4 * h, :], ACT.Square).then_inc(hg_s["sq"], 1)
                    nc.scalar.copy(Hkd[h][:, :], PS[:, 4 * h, :]).then_inc(hg_s["oc"], 1)
                    act.wait_ge(hg_s["oc"], g + 1)
                    act.sem_inc(free_act, 1)
                for h in range(2):
                    act.wait_ge(hg_s["v2"], 2 * un + h + 1)
                    o.step(A(Hln[h][:, :], Hv[h][:, :], ACT.Ln))
                o.sync()
                for h in range(2):
                    A(Hr[h][:, :], Hln[h][:, :], ACT.Exp, scale=-0.5).then_inc(hg_s["r0"], 1)
                for h in range(2):
                    g = 2 * un + h
                    act.wait_ge(hg_s["on"], g + 1)
                    nc.scalar.copy(Gh[:, g, :], Hon[:, :]).then_inc(hg_s["gh"], 1)
            for j in range(2):
                down_pair(P_HGRNO + j)
            norm(7, lambda k: LNP[:, 5, k:k + 1])
            sq_relu(P_FFN_D)
            squares(8)
            rsqrt_estimate(8)

        @block.vector
        def _(dve):
            o = Order(dve, v_ord)
            V_ = nc.vector
            TT, TS, STT = V_.tensor_tensor, V_.tensor_scalar, V_.scalar_tensor_tensor
            link, step, sync = o.link, o.step, o.sync

            def low(p, widths):
                s = p % 2
                for h in range(2):
                    dve.wait_ge(split_h, 2 * p + h + 1)
                    w = slice(h * HALF, h * HALF + widths[h])
                    TT(Wl[:, s, w], raw[:, h, 0:widths[h]], Wh[:, s, w].bitcast(F32), ALU.subtract).then_inc(split_l, 1)

            def ahead(p):
                if p + 1 < N_PAIRS:
                    low(p + 1, half_width(p + 1))

            def newton(r, v, a, b):
                link(TT(a, r, r, ALU.mult))
                link(STT(b, a, -0.5, v, ALU.mult, ALU.mult))
                link(STT(r, b, 1.5, r, ALU.add, ALU.mult))

            dve.wait_ge(consts_in, 160)
            pr = [prm[:, i, :] for i in range(24)]

            def ada(a):
                dve.wait_ge(raw_in[a % 2], 16 * (a // 2 + 1))
                for m in range(2):
                    w = raw[:, a % 2, m * D:(m + 1) * D]
                    ins = STT(w, w, 1.0, c_act[:, :], ALU.mult, ALU.mult, accum_out=MODS[:, 2 * a + m:2 * a + m + 1])
                    if m:
                        ins.then_inc(ada_used, 1)
                    else:
                        step(ins)

            def exp_acc(dst, x):
                n, r, q, m = pr[12], pr[13], pr[14], pr[15]
                link(TS(m, x, -87.3, None, ALU.is_ge))
                link(TS(r, x, -87.0, 88.0, ALU.max, ALU.min))
                link(TS(q, r, 1.0 / math.log(2.0), 12582912.0, ALU.mult, ALU.add))
                link(TS(n, q, -12582912.0, None, ALU.add))
                link(STT(r, n, -0.693359375, r, ALU.mult, ALU.add))
                link(STT(r, n, 2.12194440e-4, r, ALU.mult, ALU.add))
                link(TS(q, r, 1.0 / 5040, 1.0 / 720, ALU.mult, ALU.add))
                for cf in (1.0 / 120, 1.0 / 24, 1.0 / 6, 0.5, 1.0, 1.0):
                    link(TT(q, q, r, ALU.mult))
                    link(TS(q, q, cf, None, ALU.add))
                link(TS(prmi[:, :], n, 127.0, 8388608.0, ALU.add, ALU.mult))
                link(TT(q, q, prmi[:, :].bitcast(F32), ALU.mult))
                link(TT(dst, q, m, ALU.mult))

            lr, dt, li = pr[0], pr[1], S5A[:, 1, :]
            link(TS(lr, S5A[:, 0, :], -1e-4, None, ALU.min))
            exp_acc(dt, S5A[:, 2, :])
            link(TT(pr[2], lr, dt, ALU.mult))
            exp_acc(pr[3], pr[2])
            dve.wait_ge(s5_s["cact"], 1)
            ada(0)
            link(TT(pr[4], li, dt, ALU.mult))
            link(TS(pr[5], pr[4], 1.0 / (2 * math.pi), 12582912.0, ALU.mult, ALU.add))
            link(TS(pr[5], pr[5], -12582912.0, None, ALU.add))
            c1, c2 = 6.28125, 2 * math.pi - 6.28125
            c2h = float(np.float32(np.round(c2 * 2 ** 20) / 2 ** 20))
            link(STT(pr[6], pr[5], -c1, pr[4], ALU.mult, ALU.add))
            link(STT(pr[6], pr[5], -c2h, pr[6], ALU.mult, ALU.add))
            link(STT(pr[6], pr[5], -(c2 - c2h), pr[6], ALU.mult, ALU.add))
            link(TS(pr[6], pr[6], 3.1415925, -3.1415925, ALU.min, ALU.max))
            TS(pr[9], pr[6], 1.0, None, ALU.mult).then_inc(s5_s["prm_v"], 1)
            ada(1)
            dve.wait_ge(s5_s["prm_a"], 2)
            sin, cos = pr[10], pr[7]
            link(TT(pr[7], pr[11], pr[11], ALU.mult))
            link(TS(cos, pr[7], -2.0, 1.0, ALU.mult, ALU.add))
            ar, ai = AP_[:, 0, :, :], AP_[:, 1, :, :]
            step(V_.memset(ar[:, 0, :], 1.0))
            step(V_.memset(ai[:, 0, :], 0.0))
            step(TT(ar[:, 1, :], pr[3], cos, ALU.mult))
            link(TT(ai[:, 1, :], pr[3], sin, ALU.mult))

            def cmul(dr, di, xr, xi, yr, yi, t0, t1):
                step(TT(t0, xr, yr, ALU.mult))
                link(TT(t1, xi, yi, ALU.mult))
                link(TT(t0, t0, t1, ALU.subtract))
                step(TT(t1, xr, yi, ALU.mult))
                link(TT(di, xi, yr, ALU.mult))
                step(TT(di, di, t1, ALU.add))
                link(V_.tensor_copy(dr, t0))

            link(TS(pr[16], ar[:, 1, :], -1.0, None, ALU.add))
            step(TT(pr[17], lr, lr, ALU.mult))
            link(TT(pr[18], li, li, ALU.mult))
            link(TT(pr[17], pr[17], pr[18], ALU.add))
            link(V_.reciprocal(pr[17], pr[17]))
            step(TT(pr[18], pr[16], lr, ALU.mult))
            link(TT(pr[19], ai[:, 1, :], li, ALU.mult))
            link(TT(pr[18], pr[18], pr[19], ALU.add))
            link(TT(QP[:, 0, 0, :], pr[18], pr[17], ALU.mult))
            step(TT(pr[18], ai[:, 1, :], lr, ALU.mult))
            link(TT(pr[19], pr[16], li, ALU.mult))
            link(TT(pr[18], pr[18], pr[19], ALU.subtract))
            link(TT(QP[:, 1, 0, :], pr[18], pr[17], ALU.mult))

            def rep(x, n):
                return x.rearrange("p (o i) -> p o i", o=1).broadcast_to([P, n, 32])

            for lo, n in ((1, 1), (1, 2), (1, 4)):
                cmul(ar[:, n + 1:2 * n + 1, :], ai[:, n + 1:2 * n + 1, :], ar[:, 1:n + 1, :], ai[:, 1:n + 1, :],
                     rep(ar[:, n, :], n), rep(ai[:, n, :], n), prm[:, 12:12 + n, :], prm[:, 16:16 + n, :])
            cmul(QP[:, 0, 1:8, :], QP[:, 1, 1:8, :], ar[:, 1:8, :], ai[:, 1:8, :], rep(QP[:, 0, 0, :], 7), rep(QP[:, 1, 0, :], 7),
                 etmp[:, 0, 0:7, 0:2, :].rearrange("p m a h -> p m (a h)"), etmp[:, 1, 0:7, 0:2, :].rearrange("p m a h -> p m (a h)"))
            dve.sem_inc(s5_s["tab"], 1)
            ada(2)
            ada(3)
            step(V_.tensor_copy(tw[:, 0, :], cos))
            link(V_.tensor_copy(tw[:, 1, :], sin))
            for i in range(9):
                src = (tw[:, 0, :], tw[:, 1, :]) if i <= 3 else (PW[:, 0, i - 4, :], PW[:, 1, i - 4, :])
                dst = (tw[:, 0, :], tw[:, 1, :]) if i < 2 else (PW[:, 0, max(i - 3, 0), :], PW[:, 1, max(i - 3, 0), :])
                if i == 3:
                    continue
                step(TT(pr[12], src[0], src[0], ALU.mult))
                step(TT(pr[13], src[1], src[1], ALU.mult))
                link(TT(pr[14], src[0], src[1], ALU.mult))
                step(TT(dst[0], pr[12], pr[13], ALU.subtract))
                link(TS(dst[1], pr[14], 2.0, None, ALU.mult))
            link(TT(pr[12], pr[3], pr[3], ALU.mult))
            link(TT(pr[12], pr[12], pr[12], ALU.mult))
            link(TT(pr[12], pr[12], pr[12], ALU.mult))
            link(V_.tensor_copy(RHO[:, :, :], pr[12].rearrange("p (i o) -> p i o", o=1).broadcast_to([P, 32, NC_S5])))
            step(V_.memset(RHO[:, :, 0:1], 0.0))
            step(V_.memset(CS[:, 0, :, 0:1], 1.0))
            step(V_.memset(Xin[:, :, :, 0:1], 0.0))
            link(V_.memset(CS[:, 1, :, 0:1], 0.0))
            for k in range(6):
                n = 1 << k

                def bc(x):
                    return x.rearrange("p (i o) -> p i o", o=1).broadcast_to([P, 32, n])
                t0 = Kf[:, :, :].rearrange("p a b -> p (a b)")[:, 0:32 * n].rearrange("p (i c) -> p i c", i=32)
                t1 = U_s[:, :, :, :].rearrange("p a b c -> p (a b c)")[:, 0:32 * n].rearrange("p (i c) -> p i c", i=32)
                cmul(CS[:, 0, :, n:2 * n], CS[:, 1, :, n:2 * n], CS[:, 0, :, 0:n], CS[:, 1, :, 0:n],
                     bc(PW[:, 0, k, :]), bc(PW[:, 1, k, :]), t0, t1)
                if k in (1, 3):
                    ada(4 + k // 2)
            step(V_.memset(Kf[:, :, :], 0.0))

            dve.wait_ge(nm_mm, 8)
            TS(yg[:, :], PS[:, 7, :], RMS_EPS, None, ALU.add).then_inc(nm_v, 1)
            dve.wait_ge(nm_r0, 1)
            link(TT(yv[:, :], u_s[:, 0, :], u_s[:, 0, :], ALU.mult))
            link(STT(yv[:, :], yv[:, :], -0.5, yg[:, :], ALU.mult, ALU.mult))
            STT(Rn[:, :], yv[:, :], 1.5, u_s[:, 0, :], ALU.add, ALU.mult).then_inc(s5_s["rn"], 1)
            ada(6)
            ada(7)
            dve.wait_ge(ada_used, 8)
            link(TT(MODS[:, 0:16], MODS[:, 0:16], bada_s[:, 0:16], ALU.add))
            step(V_.tensor_copy(AB_f[:, 1, :], MODS[:, 0:8]))
            link(STT(AB_f[:, 0, :], MODS[:, 8:16], 1.0, NRM[:, 0, :], ALU.add, ALU.mult))
            dve.sem_inc(s5_s["ab"], 1)
            dve.wait_ge(s5_s["sel"], 1)
            step(V_.tensor_copy(AB_U[:, :, :].rearrange("p g a -> p (g a)"), PS[:, 1, 0:P]))
            dve.wait_ge(s5_s["ru"], 1)
            link(V_.tensor_copy(RU[:, :], PS[:, 2, 0:NC_S5]))
            dve.sem_inc(s5_s["abu"], 1)
            dve.wait_ge(x_in, 16)
            dve.wait_ge(xu_in, 16)

            def s5_u(t):
                b = t % 2
                if t >= 2:
                    dve.wait_ge(s5_s["fir"], t - 1)
                link(STT(u_s[:, b, :], X[:, t, :], AB_f[:, 0, t:t + 1], Rn[:, :], ALU.mult, ALU.mult))
                step(TS(u_s[:, b, :], u_s[:, b, :], AB_f[:, 1, t:t + 1], None, ALU.add))

            def s5_uu(t):
                if t >= 2:
                    dve.wait_ge(s5_s["inc"], t - 1)
                Ub = U_s[:, t % 2]
                link(TT(Ub, XU[:, 8 * t:8 * t + 8, :], RU[:, :].rearrange("p (o c) -> p o c", o=1).broadcast_to([P, 8, NC_S5]), ALU.mult))
                link(TT(Ub, Ub, AB_U[:, :, t:t + 1].broadcast_to([P, 8, NC_S5]), ALU.mult))
                TT(Ub, Ub, AB_U[:, :, 8 + t:9 + t].broadcast_to([P, 8, NC_S5]), ALU.add).then_inc(s5_s["u"], 1)

            def s5_kf(t):
                dve.wait_ge(s5_s["kx"], t + 1)
                if t:
                    dve.wait_ge(s5_s["fir"], t)
                for e in range(2):
                    r = slice(64 * e, 64 * e + 64)
                    ins = TT(Kf[r, :, 64 * e:64 * e + 64], PS[r, 3, :].rearrange("p (l n) -> p l n", l=8),
                             BM[r, :].rearrange("p (o n) -> p o n", o=1).broadcast_to([64, 8, 64]), ALU.mult)
                    step(ins)
                sync()
                dve.sem_inc(s5_s["kf"], 1)

            s5_uu(0)
            s5_u(0)
            s5_kf(0)
            s5_uu(1)
            fl = "p i c -> p (i c)"
            for t in range(KT):
                b = t % 2
                dve.wait_ge(s5_s["inc"], t + 1)
                co = CS[:, 0, 4 * t:4 * t + 4, :].rearrange(fl)
                si = CS[:, 1, 4 * t:4 * t + 4, :].rearrange(fl)
                Sr, Si = PS[:, 4, 0:256], PS[:, 4, 256:512]
                for dst, a_, b_ in ((0, Sr, co), (1, Si, si), (2, Si, co), (3, Sr, si)):
                    step(TT(rt[:, dst], a_, b_, ALU.mult))
                sync()
                step(TT(ZZ[:, 0], rt[:, 0], rt[:, 1], ALU.add))
                link(TT(ZZ[:, 1], rt[:, 2], rt[:, 3], ALU.subtract))
                rho = RHO[:, 4 * t:4 * t + 4, :].rearrange(fl)
                for c in range(2):
                    step(V_.tensor_tensor_scan(WW[:, c], rho, ZZ[:, c], 0.0, ALU.mult, ALU.add))
                sync()
                for dst, a_, b_ in ((0, 0, co), (1, 1, si), (2, 0, si), (3, 1, co)):
                    step(TT(rt[:, dst], WW[:, a_], b_, ALU.mult))
                sync()
                if t:
                    dve.wait_ge(s5_s["inter"], t)
                r4 = [rt[:, i].rearrange("p (i c) -> p i c", i=4) for i in range(4)]
                step(TT(Xin[:, 0, :, 1:], r4[0], r4[1], ALU.subtract))
                step(TT(Xin[:, 1, :, 1:], r4[2], r4[3], ALU.add))
                sync()
                dve.sem_inc(s5_s["xin"], 1)
                if t + 1 < KT:
                    s5_u(t + 1)
                    s5_kf(t + 1)
                ada(8 + 2 * t)
                ada(9 + 2 * t)
                if t + 2 < KT:
                    s5_uu(t + 2)
                dve.wait_ge(s5_s["y"], t + 1)
                if t:
                    dve.wait_ge(s5_s["gh"], t)
                STT(yv[:, :], u_s[:, b, :], S5D[:, t:t + 1], PS[:, 7, :], ALU.mult, ALU.add).then_inc(s5_s["yv"], 1)
                dve.wait_ge(s5_s["gh"], t + 1)
                TT(Gl[:, t, :], yg[:, :], Gh[:, t, :].bitcast(F32), ALU.subtract).then_inc(s5_s["gl"], 1)
            dve.wait_ge(ada_used, N_ADA)
            link(TT(MODS[:, 16:48], MODS[:, 16:48], bada_s[:, 16:48], ALU.add))
            link(STT(AM[:, 1, :], MODS[:, 32:40], 1.0, NRM[:, 1, :], ALU.add, ALU.mult))
            dve.sem_inc(s5_s["mods"], 1)

            low(0, half_width(0))
            for j in range(4):
                p = P_SSM + j
                ahead(p)
                for m in range(2):
                    t = 2 * j + m
                    dve.wait_ge(hid_t, t + 1)
                    v = PS[:, 4 * (p % 2) + m, :]
                    STT(tmp[:, 2 + m, :], v, MODS[:, 16 + t:17 + t], tmp[:, m, :], ALU.mult, ALU.mult).then_inc(hid_f, 1)
                    dve.wait_ge(hid_f, t + 1)
                    TT(X[:, t, :], X[:, t, :], tmp[:, 2 + m, :], ALU.add).then_inc(nm_x, 1)
                dve.sem_inc(free_dve, 1)

            def norm(n, gain, bias, eps, ln=None, last=False):
                AHEAD = 3
                bank = 4 * ((LAST[n] + 1) % 2)
                if ln is not None:
                    dve.wait_ge(nm_mean, ln + 1)
                    link(V_.tensor_copy(mu[:, :], PS[:, bank + 1, :]))
                    link(STT(nv[:, 0, :], mu[:, :], -1.0, mu[:, :], ALU.mult, ALU.mult))
                    dve.wait_ge(nm_mm, 8 * n + 8)
                    STT(nv[:, 2, :], PS[:, bank, :], eps, nv[:, 0, :], ALU.add, ALU.add).then_inc(nm_v, 1)
                else:
                    dve.wait_ge(nm_mm, 8 * n + 8)
                    TS(nv[:, 2, :], PS[:, bank, :], eps, None, ALU.add).then_inc(nm_v, 1)
                if ln is not None:
                    for k in range(AHEAD):
                        step(TT(tmp[:, k % 4, :], X[:, k, :], mu[:, :], ALU.subtract))
                dve.wait_ge(nm_r0, n + 1)
                newton(Rn[:, :], nv[:, 2, :], nv[:, 0, :], nv[:, 1, :])

                def scaled(k):
                    if ln is not None:
                        if k >= AHEAD:
                            link(TT(tmp[:, k % 4, :], X[:, k, :], mu[:, :], ALU.subtract))
                        STT(tmp[:, k % 4, :], tmp[:, k % 4, :], gain(k), Rn[:, :], ALU.mult, ALU.mult).then_inc(nm_t, 1)
                    elif bias is None:
                        STT(X[:, k, :], X[:, k, :], gain(k), Rn[:, :], ALU.mult, ALU.mult).then_inc(nm_t, 1)
                    else:
                        STT(tmp[:, k % 4, :], X[:, k, :], gain(k), Rn[:, :], ALU.mult, ALU.mult).then_inc(nm_t, 1)

                def lowp(k):
                    hh = Hh[:, k, :].bitcast(F32)
                    if ln is not None:
                        dve.wait_ge(nm_t, 8 * (n - 1) + k + 1)
                        if last:
                            TS(X[:, k, :], tmp[:, k % 4, :], bias(k), None, ALU.add).then_inc(nm_l, 1)
                            return
                        link(TS(X[:, k, :], tmp[:, k % 4, :], bias(k), None, ALU.add))
                        dve.wait_ge(nm_h, 8 * (n - 1) + k + 1)
                        TT(Hl[:, k, :], X[:, k, :], hh, ALU.subtract).then_inc(nm_l, 1)
                    elif bias is None:
                        dve.wait_ge(nm_h, 8 * (n - 1) + k + 1)
                        TT(Hl[:, k, :], X[:, k, :], hh, ALU.subtract).then_inc(nm_l, 1)
                    else:
                        dve.wait_ge(nm_h, 8 * (n - 1) + k + 1)
                        STT(Hl[:, k, :], tmp[:, k % 4, :], bias(k), hh, ALU.add, ALU.subtract).then_inc(nm_l, 1)

                scaled(0)
                for k in range(KT):
                    if k + 1 < KT:
                        scaled(k + 1)
                    lowp(k)

            hc = [8, 0]

            def hidden_out(t, g):
                dve.wait_ge(hid_h, t + 1)
                TT(Gl[:, g, :], tmp[:, t % 4, :], Gh[:, g, :].bitcast(F32), ALU.subtract).then_inc(hid_l, 1)

            def ada2(a):
                dve.wait_ge(ada2_in[a % 2], 16 * (a // 2 + 1))
                for m in range(2):
                    w = adab[:, a % 2, m * D:(m + 1) * D]
                    ins = STT(w, w, 1.0, c_act2[:, :], ALU.mult, ALU.mult, accum_out=MODS[:, 48 + 2 * a + m:49 + 2 * a + m])
                    if m:
                        ins.then_inc(ada2_used, 1)
                    else:
                        step(ins)

            def up_swiglu(p, g0):
                ahead(p)
                for m in range(2):
                    t = hc[1] + m
                    dve.wait_ge(hid_t, hc[0] + m + 1)
                    dve.wait_ge(acc_ready, 4 * p + 3 + m)
                    TT(tmp[:, t % 4, :], PS[:, 4 * (p % 2) + 2 + m, :], tmp[:, t % 4, :], ALU.mult).then_inc(hid_f, 1)
                dve.wait_ge(hid_f, 8 + hc[1] + 2)
                dve.sem_inc(free_dve, 1)
                for m in range(2):
                    hidden_out(hc[1] + m, g0 + m)
                hc[0] += 2
                hc[1] += 2

            def down(p, m0, add, final=None, ln=False):
                ahead(p)
                for m in range(4):
                    dve.wait_ge(acc_ready, 4 * p + m + 1)
                    ins = add(m0 + m, PS[:, 4 * (p % 2) + m, :])
                    if final is None:
                        step(ins)
                        continue
                    ins.then_inc(nm_x, 1)
                    k = m0 + m
                    if ln and k:
                        dve.wait_ge(nm_x, 8 * (final - 1) + k + 1)
                        sync()
                        ins = TT(nv[:, 0, :], X[:, 0, :] if k == 1 else nv[:, 0, :], X[:, k, :], ALU.add)
                        if k < KT - 1:
                            step(ins)
                        else:
                            ins.then_inc(nm_xs, 1)
                if final is None:
                    sync()
                else:
                    dve.wait_ge(nm_x, 8 * (final - 1) + m0 + 4)
                dve.sem_inc(free_dve, 1)

            def swiglu(p0, g2, n):
                p = p0
                if p0 == P_FFN_A:
                    dve.wait_ge(c2_act, 1)
                for tiles in DFF_CHUNKS0:
                    for j in range(tiles // 2):
                        up_swiglu(p, 2 * j)
                        if P_FFN_A <= p < P_FFN_A + 12:
                            ada2(2 * (p - P_FFN_A))
                            ada2(2 * (p - P_FFN_A) + 1)
                        p += 1
                    for d in range(2):
                        down(p, 4 * d, lambda k, ps: STT(X[:, k, :], ps, MODS[:, g2 + k:g2 + k + 1], X[:, k, :], ALU.mult, ALU.add),
                             n if tiles == DFF_CHUNKS0[2] else None)
                        if P_FFN_A <= p < P_FFN_A + 12:
                            ada2(2 * (p - P_FFN_A))
                            ada2(2 * (p - P_FFN_A) + 1)
                        p += 1

            def deepnorm(first):
                if first:
                    return lambda k, ps: STT(X[:, k, :], X[:, k, :], ALPHA, ps, ALU.mult, ALU.add)
                return lambda k, ps: TT(X[:, k, :], X[:, k, :], ps, ALU.add)

            def sq_relu(p0, n):
                for ci in range(4):
                    for j in range(2):
                        p = p0 + 4 * ci + j
                        ahead(p)
                        for m in range(4):
                            t = hc[1] + m
                            dve.wait_ge(hid_t, hc[0] + m + 1)
                            TT(tmp[:, t % 4, :], tmp[:, t % 4, :], tmp[:, t % 4, :], ALU.mult).then_inc(hid_f, 1)
                        dve.sem_inc(free_dve, 1)
                        for m in range(4):
                            hidden_out(hc[1] + m, 4 * j + m)
                        hc[0] += 4
                        hc[1] += 4
                    for d in range(2):
                        down(p0 + 4 * ci + 2 + d, 4 * d, deepnorm(ci == 0), n if ci == 3 else None, True)

            LAST = {1: P_FFN_A - 1, 2: P_CONV - 1, 3: P_FFN_B - 1, 4: P_ATTN - 1, 5: P_FFN_C - 1, 6: P_HGRN - 1, 7: P_FFN_D - 1, 8: N_PAIRS - 1}
            norm(1, lambda k: AM[:, 1, k:k + 1], lambda k: MODS[:, 24 + k:25 + k], RMS_EPS)
            swiglu(P_FFN_A, 40, 2)
            dve.wait_ge(late_in, 16 * 5)
            dve.wait_ge(ada2_used, N_ADA)
            link(TT(MODS[:, 48:96], MODS[:, 48:96], bada2[:, :], ALU.add))
            for n, c0 in ((2, 56), (3, 80)):
                link(STT(AM[:, n, :], MODS[:, c0:c0 + 8], 1.0, NRM[:, n, :], ALU.add, ALU.mult))
            dve.sem_inc(s5_s["mods"], 1)
            norm(2, lambda k: AM[:, 2, k:k + 1], lambda k: MODS[:, 48 + k:49 + k], RMS_EPS)
            dve.wait_ge(late_in, 16 * 5)
            TT(LB[:, 2, :], LB[:, 1, :], LB[:, 0, :], ALU.subtract).then_inc(lb_diff, 1)
            link(V_.memset(CVb[:, 0:2], 0.0))
            for j in range(8):
                p = P_CONV + j
                s = p % 2
                t = hc[1]
                ahead(p)
                dve.wait_ge(hid_t, hc[0] + 1)
                dve.wait_ge(acc_ready, 4 * p + 4)
                link(TT(CVb[:, 2:], tmp[:, 2, :], PS[:, 4 * s + 2, :], ALU.mult))
                link(TS(tmp[:, 3, :], CVb[:, 2:], CW[:, 2, j:j + 1], None, ALU.mult))
                link(STT(tmp[:, 3, :], CVb[:, 1:T + 1], CW[:, 1, j:j + 1], tmp[:, 3, :], ALU.mult, ALU.add))
                link(STT(tmp[:, 3, :], CVb[:, 0:T], CW[:, 0, j:j + 1], tmp[:, 3, :], ALU.mult, ALU.add))
                TT(tmp[:, 3, :], tmp[:, 3, :], PS[:, 4 * s, :], ALU.mult).then_inc(hid_f, 1)
                dve.wait_ge(hid_f, 8 + t + 1)
                dve.sem_inc(free_dve, 1)
                dve.wait_ge(hid_h, t + 1)
                TT(Gl[:, j, :], tmp[:, 3, :], Gh[:, j, :].bitcast(F32), ALU.subtract).then_inc(hid_l, 1)
                hc[0] += 1
                hc[1] += 1
            for j in range(2):
                down(P_CONVO + j, 4 * j, lambda k, ps: STT(X[:, k, :], ps, MODS[:, 64 + k:65 + k], X[:, k, :], ALU.mult, ALU.add), 3)
            norm(3, lambda k: AM[:, 3, k:k + 1], lambda k: MODS[:, 72 + k:73 + k], RMS_EPS)
            swiglu(P_FFN_B, 88, 4)
            norm(4, lambda k: NRM[:, 4, k:k + 1], None, RMS_EPS)

            nsw = 0
            dve.wait_ge(late_in, 16 * 9)
            for un in range(8):
                p = P_ATTN + 3 * un
                for q in range(3):
                    ahead(p + q)
                    s = (p + q) % 2
                    if q == 2:
                        dve.sem_inc(free_dve, 1)
                        continue
                    for m in range((4, 2)[q]):
                        nsw += 1
                        dve.wait_ge(at_s["swap"], nsw)
                        step(TT(tmp[:, 0, :], PS[:, 4 * s + m, :], ROT[:, 0, :], ALU.mult))
                        TT(tmp[:, 1, :], swp[:, :], ROT[:, 1, :], ALU.mult).then_inc(at_s["swf"], 1)
                        dve.wait_ge(at_s["swf"], nsw)
                        sync()
                        TT(QK[:, 4 * q + m, :], tmp[:, 0, :], tmp[:, 1, :], ALU.add).then_inc(at_s["qk"], 1)
                        dve.wait_ge(at_s["qk"], nsw)
                    dve.sem_inc(free_dve, 1)

                def head_out(h):
                    dve.wait_ge(at_s["o"], 8 * un + 4 * h + 4)
                    rows = slice(64 * h, 64 * h + 64)
                    src = PS[rows, 4 * ((p + 2) % 2) + 2 + h, :].rearrange("p (r n) -> p r n", r=4)
                    hi = Gh[rows, un, :].rearrange("p (n r) -> p r n", r=4)
                    link(V_.tensor_copy(hi, src))
                    TT(Gl[rows, un, :].rearrange("p (n r) -> p r n", r=4), src, hi.bitcast(F32), ALU.subtract).then_inc(at_s["otl"], 1)

                for g in range(8):
                    tot = 8 * un + g
                    sl = slice(g % 4, g % 4 + 1)
                    dve.wait_ge(at_s["s"], tot + 1)
                    b = 4 * (1 - (p + 2) % 2) + 2 * (g % 2)
                    link(V_.reduce_max(sm[:, 0, sl], PS[:, b:b + 2, :].rearrange("p b n -> p (b n)")[:, 0:768], AX.X))
                    TS(sm[:, 0, sl], sm[:, 0, sl], -0.125, None, ALU.mult).then_inc(at_s["max"], 1)
                    if g == 5:
                        head_out(0)
                    dve.wait_ge(at_s["p"], tot + 1)
                    link(V_.reciprocal(sm[:, 1, sl], sm[:, 1, sl]))
                    TS(Pr[:, :], Pr[:, :], sm[:, 1, sl], None, ALU.mult).then_inc(at_s["pn"], 1)
                head_out(1)
            for j in range(2):
                down(P_ATTNO + j, 4 * j, deepnorm(True), 5, True)
            norm(5, lambda k: LNP[:, 0, k:k + 1], lambda k: LNP[:, 1, k:k + 1], LN_EPS, ln=0)
            sq_relu(P_FFN_C, 6)
            norm(6, lambda k: LNP[:, 2, k:k + 1], lambda k: LNP[:, 3, k:k + 1], LN_EPS, ln=1)

            dve.wait_ge(late_in, 16 * 11)
            dve.wait_ge(lb_done, 1)
            for un in range(4):
                p = P_HGRN + 2 * un
                ahead(p)
                for h in range(2):
                    g = 2 * un + h
                    lb, oml = LB[:, 2, g:g + 1], LB[:, 3, g:g + 1]
                    dve.wait_ge(hg_s["sf"], 4 * un + 2 * h + 1)
                    TS(Hf[h][:, :], Hf[h][:, :], oml, lb, ALU.mult, ALU.add).then_inc(hg_s["f"], 1)
                    dve.wait_ge(hg_s["sf"], 4 * un + 2 * h + 2)
                    TS(Hkd[h][:, :], Hemb[h][:, :], oml, None, ALU.mult).then_inc(hg_s["k1"], 1)
                for h in range(2):
                    g = 2 * un + h
                    dve.wait_ge(hg_s["ln"], g + 1)
                    V_.tensor_tensor_scan(Hb[h][:, :], RST[:, :], Hf[h][:, :], 0.0, ALU.mult, ALU.add).then_inc(hg_s["b"], 1)
                    dve.wait_ge(hg_s["b"], g + 1)
                    bb = Hb[h][:, :].rearrange("p (c i) -> p c i", i=64)
                    TT(Hf[h][:, :].rearrange("p (c i) -> p c i", i=64), bb[:, :, 63:64].broadcast_to([P, 8, 64]), bb, ALU.subtract).then_inc(hg_s["bd"], 1)
                for h in range(2):
                    g = 2 * un + h
                    dve.wait_ge(hg_s["k1"], g + 1)
                    dve.wait_ge(hg_s["ex"], 3 * g + 3)
                    link(TT(Hke[h][:, :], Hkd[h][:, :], Hf[h][:, :], ALU.mult))
                    step(TT(Hkd[h][:, :], Hkd[h][:, :], Hemb[h][:, :], ALU.mult))
                ahead(p + 1)
                for h in range(2):
                    g = 2 * un + h
                    dve.wait_ge(hg_s["sg"], g + 1)
                    link(TT(Hq[h][:, :], PS[:, 2 + h, :], Hb[h][:, :], ALU.mult))
                    TT(Hq[h][:, :], Hq[h][:, :], Heb[h][:, :], ALU.mult).then_inc(hg_s["qd"], 1)
                    dve.wait_ge(hg_s["qd"], g + 1)
                    dve.sem_inc(hg_s["ke"], 1)
                for h in range(2):
                    g = 2 * un + h
                    dve.wait_ge(hg_s["a"], g + 1)
                    TT(Ham[h][:, :], PS[:, 4 * h, :], HM[:, :, :].rearrange("p r i -> p (r i)"), ALU.mult).then_inc(hg_s["am"], 1)
                for h in range(2):
                    g = 2 * un + h
                    dve.wait_ge(hg_s["kv"], g + 1)
                    if g:
                        dve.wait_ge(hg_s["o"], g)
                    link(V_.tensor_copy(SS[:, 0, :], PS[:, 4 * h + 2, 0:P]))
                    for c in range(1, 7):
                        ins = STT(SS[:, c, :], SS[:, c - 1, :], Heb[h][:, 64 * c + 63:64 * c + 64], PS[:, 4 * h + 2 + c % 2, (c // 2) * P:(c // 2) * P + P],
                                  ALU.mult, ALU.add)
                        if c < 6:
                            link(ins)
                        else:
                            ins.then_inc(hg_s["st"], 1)
                for h in range(2):
                    g = 2 * un + h
                    dve.wait_ge(hg_s["st"], 2 * un + 2)
                    dve.wait_ge(hg_s["ms"], g + 1)
                    TS(Hv[h][:, :], PS[:, 4 * h + 1, :], RMS_EPS, None, ALU.add).then_inc(hg_s["v2"], 1)
                    dve.wait_ge(hg_s["v2"], g + 1)
                    dve.sem_inc(free_dve, 1)
                for h in range(2):
                    g = 2 * un + h
                    dve.wait_ge(hg_s["r0"], g + 1)
                    newton(Hr[h][:, :], Hv[h][:, :], Hln[h][:, :], Hln[h][:, :])
                    dve.wait_ge(hg_s["oc"], g + 1)
                    STT(Hon[:, :], Hkd[h][:, :], HG[:, g:g + 1], Hr[h][:, :], ALU.mult, ALU.mult).then_inc(hg_s["on"], 1)
                    dve.wait_ge(hg_s["gh"], g + 1)
                    TT(Gl[:, g, :], Hon[:, :], Gh[:, g, :].bitcast(F32), ALU.subtract).then_inc(hg_s["gl"], 1)
            for j in range(2):
                down(P_HGRNO + j, 4 * j, deepnorm(True), 7, True)
            norm(7, lambda k: LNP[:, 4, k:k + 1], lambda k: LNP[:, 5, k:k + 1], LN_EPS, ln=2)
            sq_relu(P_FFN_D, 8)
            norm(8, lambda k: LNP[:, 6, k:k + 1], lambda k: LNP[:, 7, k:k + 1], LN_EPS, ln=3, last=True)

        @block.gpsimd
        def _(pool):
            g_ = nc.gpsimd
            n = [0]

            def link(ins):
                ins.then_inc(pord, 1)
                n[0] += 1
                pool.wait_ge(pord, n[0])
            pord = sem("pool_ord")
            pool.wait_ge(s5_s["tab"], 1)
            for t in range(KT):
                b = t % 2
                i0 = 4 * t
                TTg = g_.tensor_tensor
                if t >= 2:
                    pool.wait_ge(s5_s["kx"], t - 1)

                def qcoef(c):
                    return QP[:, c, :, i0:i0 + 4].rearrange("p j (i o) -> p i j o", o=1).broadcast_to([P, 4, 8, 16])

                def bmat(c):
                    return BC[:, c, i0:i0 + 4, :].rearrange("p i (o h) -> p i o h", o=1).broadcast_to([P, 4, 8, 16])
                link(TTg(ftmp[:, 0], qcoef(0), bmat(0), ALU.mult))
                link(TTg(ftmp[:, 1], qcoef(1), bmat(1), ALU.mult))
                link(TTg(Ft[:, b, 0], ftmp[:, 0], ftmp[:, 1], ALU.subtract))
                link(TTg(ftmp[:, 0], qcoef(0), bmat(1), ALU.mult))
                link(TTg(ftmp[:, 1], qcoef(1), bmat(0), ALU.mult))
                link(TTg(Ft[:, b, 1], ftmp[:, 0], ftmp[:, 1], ALU.add))
                g_.tensor_copy(Bb[:, b].rearrange("p c (i h) -> p c i h", i=4), Ft[:, b, :, :, 0, :]).then_inc(s5_s["f"], 1)

                def coef(c):
                    return AP_[:, c, :, i0:i0 + 4].rearrange("p j (i o) -> p j i o", o=1).broadcast_to([P, 9, 4, 16])

                def mat(c):
                    return BC[:, 2 + c, i0:i0 + 4, :].rearrange("p (o i) h -> p o i h", o=1).broadcast_to([P, 9, 4, 16])
                link(TTg(etmp[:, 0], coef(0), mat(0), ALU.mult))
                link(TTg(etmp[:, 1], coef(1), mat(1), ALU.mult))
                if t >= 2:
                    pool.wait_ge(s5_s["inter"], t - 1)
                link(TTg(Et[:, b, 0], etmp[:, 0], etmp[:, 1], ALU.subtract))
                link(TTg(etmp[:, 0], coef(0), mat(1), ALU.mult))
                link(TTg(etmp[:, 1], coef(1), mat(0), ALU.mult))
                link(TTg(etmp[:, 0], etmp[:, 0], etmp[:, 1], ALU.add))
                link(g_.tensor_scalar(Et[:, b, 1], etmp[:, 0], -1.0, None, ALU.mult))
                pool.sem_inc(s5_s["e"], 1)
            pool.wait_ge(split_l, 4)
            pool.dma_start(c_act2[:, :], cT).then_inc(c2_in, 16)
            for a in range(N_ADA):
                if a >= 2:
                    pool.wait_ge(ada2_used, a - 1)
                pool.dma_start(adab[:, a % 2, :], adaw[N_ADA + a]).then_inc(ada2_in[a % 2], 16)


def layout(x, c, norm1_g, norm2_g, w_ada, b_ada, ssm_a_re, ssm_a_im, ssm_log_step, ssm_b_re, ssm_b_im, ssm_c_re, ssm_c_im,
           ssm_d, ssm_w_out, conv_w_in, conv_w, conv_w_out, w_ffn_in, w_ffn_out, final_g, attn_w_in_2, attn_w_out_2,
           hgrn_w_in_2, hgrn_w_out_2, hgrn_norm_g_2, lb_logits_2, ln_mix_g_2, ln_mix_b_2, ln_ffn_g_2, ln_ffn_b_2,
           ffn_w_up_2, ffn_w_down_2):
    f = np.float32

    def col(v):
        v = np.asarray(v).reshape(*np.shape(v)[:-1], KT, P)
        return np.ascontiguousarray(np.moveaxis(v, -1, 0))

    x = np.asarray(x)[0]
    a = {}
    a["xT"] = np.ascontiguousarray(x.T.reshape(KT, P, T).transpose(1, 0, 2))
    a["xU"] = np.ascontiguousarray(x.reshape(NC_S5, CL, 64, 16)[:, ::-1].transpose(1, 3, 2, 0).reshape(P, 64, NC_S5))
    a["cT"] = np.ascontiguousarray(np.broadcast_to(np.asarray(c), (P, D)))
    a["adaw"] = np.ascontiguousarray(np.asarray(w_ada).transpose(0, 2, 1).reshape(2 * N_ADA, 2, P, D).transpose(0, 2, 1, 3).reshape(2 * N_ADA, P, HALF))
    a["bada"] = np.ascontiguousarray(np.asarray(b_ada).reshape(96, P).T)
    n1, n2 = np.asarray(norm1_g), np.asarray(norm2_g)
    a["norms"] = col(np.stack([n1[0], n2[0], n1[1], n2[1], np.asarray(final_g)]))

    def states(v):
        v = np.asarray(v)
        v = v.reshape(8, 2, 4, 64, *v.shape[2:])
        v = np.moveaxis(v, (1, 3), (0, 1))
        return np.ascontiguousarray(v.reshape(P, 32, *v.shape[4:]))
    ls = np.broadcast_to(np.asarray(ssm_log_step)[0][:, None], (64, 64))
    a["s5a"] = np.ascontiguousarray(np.stack([states(np.asarray(ssm_a_re)[0]), states(np.asarray(ssm_a_im)[0]), states(ls)], 1))
    a["s5bc"] = np.ascontiguousarray(np.stack([states(np.asarray(ssm_b_re)[0]), states(np.asarray(ssm_b_im)[0]),
                                               states(np.asarray(ssm_c_re)[0].transpose(0, 2, 1)), states(np.asarray(ssm_c_im)[0].transpose(0, 2, 1))], 1))
    a["s5d"] = col(np.asarray(ssm_d)[0])

    pairs = []

    def add(w):
        k = w.shape[0] // P
        n = w.shape[1]
        w = w.reshape(k, P, n).transpose(1, 0, 2)
        blk = np.zeros((P, 2, HALF), f)
        blk[:, 0, :4 * n] = w[:, 0:4].reshape(P, -1)
        blk[:, 1, :(k - 4) * n] = w[:, 4:].reshape(P, -1)
        pairs.append(blk.reshape(P, 2 * HALF))

    wo = np.asarray(ssm_w_out)[0]
    for j in range(4):
        add(np.concatenate([wo[:, 256 * j:256 * j + 256], wo[:, D + 256 * j:D + 256 * j + 256]], 1))

    def swiglu(wi, wd):
        h = 0
        for tiles in DFF_CHUNKS0:
            for j in range(tiles // 2):
                c0 = h + 256 * j
                add(np.concatenate([wi[:, c0:c0 + 256], wi[:, FFN0 + c0:FFN0 + c0 + 256]], 1))
            for d_ in range(2):
                add(wd[h:h + tiles * P, 512 * d_:512 * d_ + 512])
            h += tiles * P
    swiglu(np.asarray(w_ffn_in)[0], np.asarray(w_ffn_out)[0])
    wc = np.asarray(conv_w_in)[0].reshape(D, 3, 8, P)
    for j in range(8):
        add(wc[:, :, j].reshape(D, 384))
    for j in range(2):
        add(np.asarray(conv_w_out)[0][:, 512 * j:512 * j + 512])
    swiglu(np.asarray(w_ffn_in)[1], np.asarray(w_ffn_out)[1])
    wa = np.asarray(attn_w_in_2)[0].reshape(D, 3, 3, 8, P)
    for un in range(8):
        add(np.concatenate([wa[:, 0, 0, un], wa[:, 0, 1, un], wa[:, 1, 0, un], wa[:, 1, 1, un]], 1))
        add(np.concatenate([wa[:, 2, 0, un], wa[:, 2, 1, un]], 1))
        add(np.concatenate([wa[:, 0, 2, un], wa[:, 1, 2, un], wa[:, 2, 2, un]], 1))
    for j in range(2):
        add(np.asarray(attn_w_out_2)[0][:, 512 * j:512 * j + 512])

    def sq_relu(wu, wd):
        for ci in range(4):
            for j in range(2):
                add(wu[:, 1024 * ci + 512 * j:1024 * ci + 512 * j + 512])
            for j in range(2):
                add(wd[1024 * ci:1024 * ci + 1024, 512 * j:512 * j + 512])
    sq_relu(np.asarray(ffn_w_up_2)[0], np.asarray(ffn_w_down_2)[0])
    wh = np.asarray(hgrn_w_in_2)[0].reshape(D, 3, 4, 256)
    for un in range(4):
        add(np.concatenate([wh[:, 1, un], wh[:, 0, un]], 1))
        add(np.ascontiguousarray(wh[:, 2, un]))
    for j in range(2):
        add(np.asarray(hgrn_w_out_2)[0][:, 512 * j:512 * j + 512])
    sq_relu(np.asarray(ffn_w_up_2)[1], np.asarray(ffn_w_down_2)[1])
    a["wstream"] = np.stack(pairs)

    a["convw"] = col(np.asarray(conv_w)[0])
    mg, mb, fg, fb = (np.asarray(v) for v in (ln_mix_g_2, ln_mix_b_2, ln_ffn_g_2, ln_ffn_b_2))
    a["lnp"] = col(np.stack([mg[0], mb[0], fg[0], fb[0], mg[1], mb[1], fg[1], fb[1]]))
    a["hgn"] = col(np.asarray(hgrn_norm_g_2)[0])
    a["lbl"] = col(np.asarray(lb_logits_2))

    i = np.arange(P)
    inv = 10000.0 ** (-np.arange(32, dtype=f) * f(2.0 / 64))
    ang = (np.arange(T, dtype=f)[:, None] * inv.astype(f)[None, :]).astype(f)
    cosr, sinr = np.cos(ang).astype(f).T, np.sin(ang).astype(f).T
    a["rot"] = np.ascontiguousarray(np.stack([np.tile(cosr, (4, 1)), np.concatenate([-sinr, sinr, -sinr, sinr])], 1))
    m = np.zeros((P, 4 * 512 + 256 + P), f)
    for r in range(4):
        dist = (4 * i + r)[:, None] - np.arange(512)[None, :]
        blk = (4 * i + r) // P
        ok = (dist >= 0) & (dist <= P)
        m[:, 512 * r:512 * r + 512] = np.where(ok, 0.0, NEG)
    d1 = i[:, None] - i[None, :]
    m[:, 2048:2048 + P] = np.where(d1 >= 0, 0.0, NEG)
    m[:, 2048 + P:2048 + 2 * P] = np.where((d1 >= 0) & (d1 % 4 == 0), 0.0, NEG)
    m[:, 2304:] = np.eye(P)
    a["masks"] = (m.view(np.uint32) >> 16).astype(np.uint16)
    h = np.zeros((P, 4 * P + T + 64), f)
    hm = ((i[:, None] <= i[None, :]) & (i[:, None] // 64 == i[None, :] // 64)).astype(f)
    h[:, 0:4 * P] = np.tile(hm, (1, 4))
    h[:, 4 * P:4 * P + T] = (np.arange(T) % 64 != 0).astype(f)[None]
    h[:, 4 * P + T:] = (((i % 64) // 16)[:, None] == (np.arange(64) // 16)[None, :]).astype(f)
    a["hmask"] = h
    a["consts"] = np.concatenate([np.eye(P, dtype=f), np.full((P, P), 1.0 / D, f), np.full((P, P), 1.0 / P, f)], 1)
    js = np.zeros((1, 8, P), f)
    gs = np.zeros((P, 8, P), f)
    for j in range(8):
        js[0, j, 16 * (7 - j):16 * (7 - j) + 16] = 1
        for hh in range(16):
            gs[16 * j + hh, j, hh::16] = 1
    a["jsel"], a["gsel"] = js, gs
    return a


NAMES = ["xT", "xU", "cT", "adaw", "bada", "norms", "s5a", "s5bc", "s5d", "wstream", "convw", "lnp", "hgn", "lbl",
         "rot", "masks", "hmask", "consts", "jsel", "gsel"]


def kernel(**inputs):
    import concourse.bacc as bacc
    from concourse.bass_utils import run_bass_kernel_spmd

    arrays = layout(**inputs)
    nc = bacc.Bacc("TRN2", target_bir_lowering=False, num_devices=1)
    feed, args = {}, []
    for name in NAMES:
        arr = arrays[name]
        feed[name] = arr
        args.append(nc.dram_tensor(name, arr.shape, mybir.dt.from_np(arr.dtype), kind="ExternalInput").ap())
    o = nc.dram_tensor("yT", (P, KT, T), F32, kind="ExternalOutput").ap()
    build(nc, *args, o)
    res = run_bass_kernel_spmd(nc, [feed], core_ids=[0])
    y = res.results[0]["yT"]
    return np.ascontiguousarray(y.transpose(1, 0, 2).reshape(D, T).T).reshape(1, T, D)
```
